# Optimizing a Trainium2 kernel written in Bass

```python
import math
import jax, jax.numpy as jnp
from jax import lax
import numpy as np

D_MODEL = 2048
BATCH = 1
SEQ = 256
DEPTH = 1

RET_HEADS = 8
RET_DK = 128
RET_DV = 256
RET_CHUNK = 128
ROPE_BASE = 10000.0
MOBA_HEADS = 16
MOBA_HD = 128
MOBA_BLOCK = 256
MOBA_TOPK = 3
MOBA_Q_CHUNK = 64
D_FF = 5632
CONV_WIDTH = 3
NORM_EPS = 1e-6
GN_EPS = 1e-5

RET_QK_W = RET_HEADS * RET_DK
RET_V_W = RET_HEADS * RET_DV
MOBA_W = MOBA_HEADS * MOBA_HD
IN_SPLITS = (RET_QK_W, RET_QK_W, RET_V_W, RET_V_W, MOBA_W, MOBA_W, MOBA_W, D_MODEL, D_MODEL)
IN_WIDTH = sum(IN_SPLITS)
IN_OFFSETS = [int(o) for o in np.cumsum(IN_SPLITS)[:-1]]

kernel_name = "hybrid_retention_moba_convffn_block"

def rms_norm(x, w):
    xf = x.astype(jnp.float32)
    y = xf * lax.rsqrt(jnp.mean(xf * xf, axis=-1, keepdims=True) + NORM_EPS)
    return (y * w.astype(jnp.float32)).astype(x.dtype)

def rotary(x, pos):
    half = x.shape[-1] // 2
    inv = ROPE_BASE ** (-jnp.arange(half, dtype=jnp.float32) / half)
    ang = pos.astype(jnp.float32)[:, None] * inv[None, :]
    cos = jnp.cos(ang)[None, :, None, :]
    sin = jnp.sin(ang)[None, :, None, :]
    x1, x2 = x[..., :half], x[..., half:]
    return jnp.concatenate([x1 * cos - x2 * sin, x1 * sin + x2 * cos], axis=-1)

def retention(q, k, v):
    B, S, H, dk = q.shape
    dv = v.shape[-1]
    C = RET_CHUNK
    N = S // C
    f32 = jnp.float32
    log_g = jnp.log1p(-jnp.exp2(-5.0 - jnp.arange(H, dtype=f32)))
    q = q.astype(f32).reshape(B, N, C, H, dk)
    k = (k.astype(f32) * (dk ** -0.5)).reshape(B, N, C, H, dk)
    v = v.astype(f32).reshape(B, N, C, H, dv)
    idx = jnp.arange(C)
    diff = idx[:, None] - idx[None, :]
    dec = jnp.where(diff[None] >= 0,
                    jnp.exp(jnp.maximum(diff, 0).astype(f32)[None] * log_g[:, None, None]), 0.0)
    s = jnp.einsum('bnihd,bnjhd->bnhij', q, k) * dec[None, None]
    inner = jnp.einsum('bnhij,bnjhe->bnihe', s, v)
    zeta = jnp.exp((C - 1 - idx).astype(f32)[None, :] * log_g[:, None])
    kv = jnp.einsum('bnjhd,bnjhe->bnhde', k * zeta.T[None, None, :, :, None], v)
    g_chunk = jnp.exp(C * log_g)[None, :, None, None]

    def step(R, kv_n):
        return R * g_chunk + kv_n, R

    _, R_prev = lax.scan(step, jnp.zeros((B, H, dk, dv), f32), jnp.moveaxis(kv, 1, 0))
    R_prev = jnp.moveaxis(R_prev, 0, 1)
    xi = jnp.exp((idx + 1).astype(f32)[None, :] * log_g[:, None])
    cross = jnp.einsum('bnihd,bnhde->bnihe', q * xi.T[None, None, :, :, None], R_prev)
    return (inner + cross).reshape(B, S, H, dv)

def group_norm_heads(o):
    mu = jnp.mean(o, axis=-1, keepdims=True)
    var = jnp.mean(jnp.square(o - mu), axis=-1, keepdims=True)
    return (o - mu) * lax.rsqrt(var + GN_EPS)

def moba_attention(q, k, v):
    B, S, H, hd = q.shape
    dtype = q.dtype
    nb = -(-S // MOBA_BLOCK)
    pad = nb * MOBA_BLOCK - S
    kp = jnp.pad(k, ((0, 0), (0, pad), (0, 0), (0, 0))).reshape(B, nb, MOBA_BLOCK, H, hd)
    vp = jnp.pad(v, ((0, 0), (0, pad), (0, 0), (0, 0))).reshape(B, nb, MOBA_BLOCK, H, hd)
    k_mean = jnp.mean(kp.astype(jnp.float32), axis=2)
    kbh = jnp.transpose(kp, (0, 3, 1, 2, 4))
    vbh = jnp.transpose(vp, (0, 3, 1, 2, 4))
    n_sel = min(MOBA_TOPK, nb - 1)
    scale = 1.0 / math.sqrt(hd)
    QC = MOBA_Q_CHUNK
    nq = S // QC
    qc = jnp.moveaxis(q.reshape(B, nq, QC, H, hd), 1, 0)
    b_ix = jnp.arange(B)[:, None, None, None]
    h_ix = jnp.arange(H)[None, :, None, None]

    def step(args):
        qi, ci = args
        q_pos = ci * QC + jnp.arange(QC)
        qblk = (ci * QC) // MOBA_BLOCK
        k_own = lax.dynamic_index_in_dim(kp, qblk, axis=1, keepdims=False)
        v_own = lax.dynamic_index_in_dim(vp, qblk, axis=1, keepdims=False)
        k_pos = qblk * MOBA_BLOCK + jnp.arange(MOBA_BLOCK)
        s_own = jnp.einsum('bqhd,bkhd->bhqk', qi, k_own).astype(jnp.float32) * scale
        s_own = jnp.where((k_pos[None, :] <= q_pos[:, None])[None, None], s_own, -jnp.inf)
        if n_sel > 0:
            gate = jnp.einsum('bqhd,bnhd->bhqn', qi.astype(jnp.float32), k_mean)
            gate = jnp.where((jnp.arange(nb) < qblk)[None, None, None], gate, -jnp.inf)
            _, sel = lax.top_k(gate, n_sel)
            valid = sel < qblk
            k_sel = kbh[b_ix, h_ix, sel]
            v_sel = vbh[b_ix, h_ix, sel]
            s_sel = jnp.einsum('bqhd,bhqskd->bhqsk', qi, k_sel).astype(jnp.float32) * scale
            s_sel = jnp.where(valid[..., None], s_sel, -jnp.inf).reshape(B, H, QC, n_sel * MOBA_BLOCK)
            p = jax.nn.softmax(jnp.concatenate([s_own, s_sel], axis=-1), axis=-1).astype(dtype)
            p_own = p[..., :MOBA_BLOCK]
            p_sel = p[..., MOBA_BLOCK:].reshape(B, H, QC, n_sel, MOBA_BLOCK)
            o = (jnp.einsum('bhqk,bkhd->bqhd', p_own, v_own)
                 + jnp.einsum('bhqsk,bhqskd->bqhd', p_sel, v_sel))
        else:
            p_own = jax.nn.softmax(s_own, axis=-1).astype(dtype)
            o = jnp.einsum('bhqk,bkhd->bqhd', p_own, v_own)
        return o

    out = lax.map(step, (qc, jnp.arange(nq)))
    return jnp.moveaxis(out, 0, 1).reshape(B, S, H, hd)

def token_mixer(u, w_in, ret_w_o, moba_w_o, w_out):
    B, S, _ = u.shape
    dtype = u.dtype
    proj = u @ w_in
    rq, rk, rv, rg, mq, mk, mv, ga, gb = jnp.split(proj, IN_OFFSETS, axis=-1)
    pos = jnp.arange(S)
    rq = rotary(rq.astype(jnp.float32).reshape(B, S, RET_HEADS, RET_DK), pos)
    rk = rotary(rk.astype(jnp.float32).reshape(B, S, RET_HEADS, RET_DK), pos)
    o_ret = group_norm_heads(retention(rq, rk, rv.reshape(B, S, RET_HEADS, RET_DV)))
    o_ret = (jax.nn.silu(rg.astype(jnp.float32)) * o_ret.reshape(B, S, RET_V_W)).astype(dtype)
    y_ret = o_ret @ ret_w_o
    o_moba = moba_attention(mq.reshape(B, S, MOBA_HEADS, MOBA_HD),
                            mk.reshape(B, S, MOBA_HEADS, MOBA_HD),
                            mv.reshape(B, S, MOBA_HEADS, MOBA_HD))
    y_moba = o_moba.reshape(B, S, MOBA_W) @ moba_w_o
    merged = jax.nn.sigmoid(ga) * y_ret + jax.nn.sigmoid(gb) * y_moba
    return merged @ w_out

def conv_ffn(u, w_up, conv_w, conv_b, w_down):
    S = u.shape[1]
    h = u @ w_up
    hp = jnp.pad(h, ((0, 0), (CONV_WIDTH - 1, 0), (0, 0)))
    h = sum(hp[:, i:i + S] * conv_w[i] for i in range(CONV_WIDTH)) + conv_b
    a, b = jnp.split(h, 2, axis=-1)
    return (jax.nn.silu(a) * b) @ w_down

def setup_inputs(seed: int = 0) -> dict:
    key = jax.random.key(seed)
    ks = jax.random.split(key, 18)
    f32 = jnp.float32
    L, D = DEPTH, D_MODEL

    def nrm(k, shape, scale):
        return jax.random.normal(k, shape, f32) * scale

    return {
        "x": nrm(ks[0], (BATCH, SEQ, D), 1.0),
        "c": nrm(ks[1], (BATCH, D), 1.0),
        "ada_w": nrm(ks[2], (L, D, 6 * D), 0.01),
        "ada_b": nrm(ks[3], (L, 6 * D), 0.01),
        "mix_norm_pre": 1.0 + nrm(ks[4], (L, D), 0.05),
        "mix_norm_post": 1.0 + nrm(ks[5], (L, D), 0.05),
        "w_in": nrm(ks[6], (L, D, IN_WIDTH), D ** -0.5),
        "ret_w_o": nrm(ks[7], (L, RET_V_W, D), RET_V_W ** -0.5),
        "moba_w_o": nrm(ks[8], (L, MOBA_W, D), MOBA_W ** -0.5),
        "w_out": nrm(ks[9], (L, D, D), D ** -0.5),
        "ffn_norm_pre": 1.0 + nrm(ks[10], (L, D), 0.05),
        "ffn_norm_post": 1.0 + nrm(ks[11], (L, D), 0.05),
        "ffn_w_up": nrm(ks[12], (L, D, 2 * D_FF), D ** -0.5),
        "ffn_conv_w": nrm(ks[13], (L, CONV_WIDTH, 2 * D_FF), CONV_WIDTH ** -0.5),
        "ffn_conv_b": nrm(ks[14], (L, 2 * D_FF), 0.01),
        "ffn_w_down": nrm(ks[15], (L, D_FF, D), D_FF ** -0.5),
    }

def reference(x, c, ada_w, ada_b, mix_norm_pre, mix_norm_post, w_in, ret_w_o, moba_w_o, w_out,
              ffn_norm_pre, ffn_norm_post, ffn_w_up, ffn_conv_w, ffn_conv_b, ffn_w_down):
    c_act = jax.nn.silu(c)
    for l in range(DEPTH):
        mod = c_act @ ada_w[l] + ada_b[l]
        sh1, sc1, g1, sh2, sc2, g2 = [m[:, None, :] for m in jnp.split(mod, 6, axis=-1)]
        u = rms_norm(x, mix_norm_pre[l]) * (1.0 + sc1) + sh1
        y = token_mixer(u, w_in[l], ret_w_o[l], moba_w_o[l], w_out[l])
        x = x + (1.0 + g1) * rms_norm(y, mix_norm_post[l])
        u = rms_norm(x, ffn_norm_pre[l]) * (1.0 + sc2) + sh2
        y = conv_ffn(u, ffn_w_up[l], ffn_conv_w[l], ffn_conv_b[l], ffn_w_down[l])
        x = x + (1.0 + g2) * rms_norm(y, ffn_norm_post[l])
    return x


_drawn_inputs = setup_inputs


def setup_inputs(seed=0):
    import zlib

    import numpy as np

    out = dict(_drawn_inputs(seed))
    spreads = {}
    factors = {'ffn_conv_b': 7.379}
    for name, (base, spread) in spreads.items():
        noise = np.random.default_rng([zlib.crc32(name.encode()), seed]).standard_normal(out[name].shape)
        drawn = base * np.exp(spread * noise) if base else spread * noise
        out[name] = __import__('jax').numpy.asarray(drawn.astype(out[name].dtype))
    for name, factor in factors.items():
        out[name] = (out[name] * factor).astype(out[name].dtype)
    return out
```

```python
import math
from contextlib import ExitStack

import numpy as np

import concourse.bass as bass
from concourse import mybir

F32 = mybir.dt.float32
F32R = mybir.dt.float32r
ALU = mybir.AluOpType
ACT = mybir.ActivationFunctionType
AX = mybir.AxisListType

P = 128
SEQ, D = 256, 2048
T = SEQ // P
KT = D // P
RET_HEADS, RET_DK, RET_DV = 8, 128, 256
MOBA_HEADS, MOBA_HD = 16, 128
D_FF = 5632
NORM_EPS, GN_EPS = 1e-6, 1e-5
ROPE_BASE = 10000.0
NC = 512
KB = 4
HB = 8
SETH = 4
COL_RQ, COL_RK, COL_RV, COL_RG, COL_MQ, COL_MK, COL_MV, COL_GA, COL_GB = (
    0, 1024, 2048, 4096, 6144, 8192, 10240, 12288, 14336)
RET_SETS = RET_HEADS // SETH
MOBA_SETS = MOBA_HEADS // SETH
G_MOBA = 6 * RET_SETS
G_GA = G_MOBA + 4 * MOBA_SETS
G_RETO = G_GA + 4
G_MOBAO = G_RETO + 4
G_OUT = G_MOBAO + 4
G_UP = G_OUT + 4
UPS = D_FF // (2 * P)
G_DOWN = G_UP + UPS
DOWNS = D_FF // (KB * P)
ADA_BG = 256
MASKED = -1.7e38


def hybrid_block(nc, x, c, ada_w, ada_b, mix_norm_pre, mix_norm_post, w_in, ret_w_o, moba_w_o, w_out,
                 ffn_norm_pre, ffn_norm_post, ffn_w_up, ffn_conv_w, ffn_conv_b, ffn_w_down,
                 identity, rope_cos, rope_sin, causal, decay_dram, out):
    ctx = ExitStack()

    def sb(name, shape, dt=F32, stack=ctx):
        return stack.enter_context(nc.sbuf_tensor(name, shape, dt))

    def sem(name):
        return ctx.enter_context(nc.semaphore(name))

    def shared(*plans):
        made = {}
        for plan in plans:
            with ExitStack() as part:
                for name, shape, dt in plan:
                    made[name] = sb(name, shape, dt, part)
        return made

    def hold(name, kib4):
        sb(name, [P, kib4])

    with ctx:
        stage = sb("stage", [P, 4, KB, NC])
        w_high = sb("w_high", [P, 4, 2, NC], F32R)
        w_low = sb("w_low", [P, 4, 2, NC], F32R)
        lhs = sb("lhs", [P, KT, 2 * SEQ], F32R)
        ident = sb("ident", [P, P])
        ones = sb("ones", [P, P])
        cos2 = sb("cos2", [P, T, P])
        sin2 = sb("sin2", [P, T, P])
        mask = sb("mask", [P, 3 * P])
        cols = sb("cols", [P, 7 * KT])
        c_act = sb("c_act", [P, KT])
        scale1 = sb("scale1", [P, KT])
        shift1 = sb("shift1", [P, KT])
        scale2 = sb("scale2", [P, KT])
        shift2 = sb("shift2", [P, KT])
        gain = sb("gain", [P, KT])
        post_cols = sb("post_cols", [P, 4 * KT])
        ada_cols = sb("ada_cols", [P, 4 * KT])
        conv_cols = sb("conv_cols", [P, 4, 88])
        stats = sb("stats", [P, 4, 6])
        moments = sb("moments", [P, 4, 2])
        inv_std = sb("inv_std", [P, 4])
        row_max = sb("row_max", [P, 2 * SETH])
        neg_max = sb("neg_max", [P, 2 * SETH])
        row_sum = sb("row_sum", [P, 2 * SETH])
        inv_sum = sb("inv_sum", [P, 2 * SETH])
        squares = sb("squares", [P, T, 4])
        mean_sq = sb("mean_sq", [P, T])
        rstd = sb("rstd", [P, T])

        m = shared([("x_sb", [P, T, D], F32)],
                   [("gate_b", [P, T, D], F32)])
        x_sb, gate_b = m["x_sb"], m["gate_b"]
        hold("hold_x", T * D)
        rest = ExitStack()
        m = {}

        def region(name, size, *plans):
            m.update(shared(*plans))
            sb(name, [P, size], F32, rest)

        region("hold_m", 4096,
               [("v_ret", [P, T, 1024], F32), ("o_ret", [P, T, 1024], F32)],
               [("src_b", [P, KT, SEQ], F32)])
        region("hold_r", 4096, [("src_a", [P, KT, SEQ], F32)])
        ffn_at = None
        region("hold_q", 8192,
               [("rot", [P, T, NC], F32), ("rot_cos", [P, NC], F32), ("rot_sin", [P, NC], F32),
                ("qT_ret", [P, SETH, SEQ], F32), ("kT_ret", [P, SETH, SEQ], F32),
                ("sT0", [P, SETH, SEQ], F32), ("sT1", [P, SETH, P], F32)],
               [("gate_a", [P, T, D], F32),
                ("qk_nat", [P, T, NC], F32), ("qT", [P, SETH, SEQ], F32),
                ("kT", [P, SETH, SEQ], F32), ("v_moba", [P, T, NC], F32)],
               [("ada_first", [P, 4, KB, NC], F32)])
        region("hold_d", 3072,
               [("decay", [P, RET_HEADS, SEQ], F32), ("gate_r", [P, T, NC], F32)],
               [("p0", [P, SETH, P], F32), ("p1", [P, SETH, SEQ], F32),
                ("pTa", [P, SETH, SEQ], F32), ("pTb", [P, SETH, P], F32)],
               [("rows", [7 * KT, P], F32), ("post_rows", [4 * KT, P], F32), ("conv_rows", [88, 4, P], F32)])
        region("hold_a", 2560,
               [("ada_ring", [P, 2, KB, ADA_BG], F32), ("ada_acc", [P, 2, ADA_BG], F32)],
               [("ada_acc1", [P, 2, 2, NC], F32)])
        rest.close()
        m.update(shared(
            [("gain_b", [P, D], F32), ("y_gain", [P, T, D], F32),
             ("gT", [P, D_FF // P, SEQ], F32), ("g_lhs", [P, 2, KB, 2 * SEQ], F32R)]))
        with ExitStack() as part:
            sb("skip_gain", [P, D], F32, part)
            for name, shape in (("h_pad", [P, 4, SEQ + 2]), ("h_conv", [P, 4, SEQ]),
                                ("h_low", [P, 4, SEQ]), ("a_act", [P, 2, SEQ])):
                m[name] = sb(name, shape, F32, part)
        v_ret, o_ret, src_b, src_a = m["v_ret"], m["o_ret"], m["src_b"], m["src_a"]
        rot, rot_cos, rot_sin, qT_ret, kT_ret = m["rot"], m["rot_cos"], m["rot_sin"], m["qT_ret"], m["kT_ret"]
        sT0, sT1, gate_a, qk_nat, qT, kT = m["sT0"], m["sT1"], m["gate_a"], m["qk_nat"], m["qT"], m["kT"]
        v_moba, ada_first, decay, gate_r = m["v_moba"], m["ada_first"], m["decay"], m["gate_r"]
        p0, p1, pTa, pTb = m["p0"], m["p1"], m["pTa"], m["pTb"]
        rows, post_rows, conv_rows = m["rows"], m["post_rows"], m["conv_rows"]
        ada_ring, ada_acc, ada_acc1 = m["ada_ring"], m["ada_acc"], m["ada_acc1"]
        gain_b, y_gain, gT, g_lhs = m["gain_b"], m["y_gain"], m["gT"], m["g_lhs"]
        h_pad, h_conv, h_low, a_act = m["h_pad"], m["h_conv"], m["h_low"], m["a_act"]

        ps = ctx.enter_context(nc.psum_tensor("ps", [P, 8, NC], F32))

        loaded = [sem(f"loaded{b}") for b in range(4)]
        high_ready = sem("high_ready")
        split_ready = sem("split_ready")
        used = sem("used")
        lhs_high = sem("lhs_high")
        lhs_ready = sem("lhs_ready")
        rows_in = sem("rows_in")
        x_in = [sem("x_in0"), sem("x_in1")]
        consts_in = sem("consts_in")
        ident_in = sem("ident_in")
        decay_in = sem("decay_in")
        ones_set = sem("ones_set")
        cols_turned = sem("cols_turned")
        cols_ready = sem("cols_ready")
        squared = sem("squared")
        norm_sum = sem("norm_sum")
        norm_mean = sem("norm_mean")
        norm_root = sem("norm_root")
        norm_inv = sem("norm_inv")
        x_scaled = sem("x_scaled")
        x_turned = sem("x_turned")
        xT_ready = sem("xT_ready")
        ada1_in = [sem(f"ada1_in{b}") for b in range(4)]
        ada1_step = sem("ada1_step")
        ada1_summed = sem("ada1_summed")
        ada1_cols = sem("ada1_cols")
        mod1 = sem("mod1")
        u_ready = sem("u_ready")
        ada_in = [sem("ada_in0"), sem("ada_in1")]
        ada_step = sem("ada_step")
        ada_summed = sem("ada_summed")
        ada_kept = sem("ada_kept")
        rot_terms = sem("rot_terms")
        rot_ready = sem("rot_ready")
        rqk_turned = sem("rqk_turned")
        rqk_ready = sem("rqk_ready")
        ret_scored = sem("ret_scored")
        ret_decayed = sem("ret_decayed")
        rv_ready = sem("rv_ready")
        ret_summed = sem("ret_summed")
        gn_stats = sem("gn_stats")
        gn_moments = sem("gn_moments")
        gn_var = sem("gn_var")
        gn_root = sem("gn_root")
        gn_inv = sem("gn_inv")
        gn_ready = sem("gn_ready")
        rg_ready = sem("rg_ready")
        ret_gated = sem("ret_gated")
        ret_turned = sem("ret_turned")
        ret_kept = sem("ret_kept")
        mqk_nat = sem("mqk_nat")
        mqk_turned = sem("mqk_turned")
        mqk_ready = sem("mqk_ready")
        scored = sem("scored")
        masked = sem("masked")
        maxed = sem("maxed")
        neg_ready = sem("neg_ready")
        exp_ready = sem("exp_ready")
        inv_ready = sem("inv_ready")
        probs_ready = sem("probs_ready")
        probs_turned = sem("probs_turned")
        probsT_ready = sem("probsT_ready")
        mv_ready = sem("mv_ready")
        attended = sem("attended")
        att_kept = sem("att_kept")
        gate_ready = sem("gate_ready")
        gated = sem("gated")
        merge_turned = sem("merge_turned")
        merge_kept = sem("merge_kept")
        gain_col = sem("gain_col")
        gain_diag = sem("gain_diag")
        gain_spread = sem("gain_spread")
        gain_ready = sem("gain_ready")
        x_back = sem("x_back")
        y_squared = sem("y_squared")
        y_gained = sem("y_gained")
        x2_ready = sem("x2_ready")
        x2_squared = sem("x2_squared")
        x2_scaled = sem("x2_scaled")
        x2_turned = sem("x2_turned")
        u2_ready = sem("u2_ready")
        mod2 = sem("mod2")
        pad_set = sem("pad_set")
        up_low = sem("up_low")
        up_sum = sem("up_sum")
        conv_step = sem("conv_step")
        a_ready = sem("a_ready")
        g_ready = sem("g_ready")
        g_high = sem("g_high")
        g_split = sem("g_split")
        y2_squared = sem("y2_squared")
        y2_gained = sem("y2_gained")
        out_ready = sem("out_ready")
        stored = sem("stored")

        block = ctx.enter_context(nc.Block())

        diag1 = src_b[:, KT // 2:KT, :].rearrange("p k n -> p (k n)")
        diag2 = y_gain[:, 0, :]

        def wait(engine, semaphore, value):
            if not isinstance(value, int) or value > 0:
                engine.wait_ge(semaphore, value)

        def moba_out_of_psum(s, g):
            return ((mqk_nat, 4 * s + 2), (mqk_nat, 4 * s + 4), (mv_ready, 2 * s + 2), (gate_ready, 2 * s + 2))[g]

        def out_of_psum(G):
            if G < 0:
                return None
            if G < G_MOBA:
                s, g = divmod(G, 6)
                return ((rot_ready, 4 * s + 2), (rot_ready, 4 * s + 4), (rv_ready, 4 * s + 2),
                        (rv_ready, 4 * s + 4), (rg_ready, 2 * s + 1), (rg_ready, 2 * s + 2))[g]
            if G < G_GA:
                return moba_out_of_psum(*divmod(G - G_MOBA, 4))
            phase, n = divmod(G - G_GA, 4)
            return ((gate_ready, 2 * MOBA_SETS + 2 * n + 2), (gated, 2 * n + 2), (gated, 8 + 3 * n + 2),
                    (y_gained, 2 * n + 2))[phase]

        def w_tile(w, kb, col):
            return w[0, kb * KB * P:(kb + 1) * KB * P, bass.ds(col, NC)].rearrange("(k p) n -> p k n", p=P)

        @block.sync
        def _(sp):
            for n, src in enumerate((c[0], mix_norm_pre[0], ffn_norm_pre[0], ada_b[0, 0:D], ada_b[0, D:2 * D],
                                     ada_b[0, 3 * D:4 * D], ada_b[0, 4 * D:5 * D])):
                sp.dma_start(rows[n * KT:(n + 1) * KT, :], src.rearrange("(k p) -> k p", p=P)).then_inc(rows_in, 16)
            for n, src in enumerate((mix_norm_post[0], ffn_norm_post[0], ada_b[0, 2 * D:3 * D], ada_b[0, 5 * D:6 * D])):
                sp.dma_start(post_rows[n * KT:(n + 1) * KT, :],
                             src.rearrange("(k p) -> k p", p=P)).then_inc(rows_in, 16)
            for n in range(3):
                sp.dma_start(conv_rows[:, n, :], ffn_conv_w[0, n].rearrange("(k p) -> k p", p=P)).then_inc(rows_in, 16)
            sp.dma_start(conv_rows[:, 3, :], ffn_conv_b[0].rearrange("(k p) -> k p", p=P)).then_inc(rows_in, 16)
            for t in range(T):
                sp.dma_start(x_sb[:, t, :], x[0, t * P:(t + 1) * P, :]).then_inc(x_in[t], 16)

            def first_chunk(kb, which, n):
                for b in range(4):
                    if not (isinstance(n, int) and n == 0):
                        sp.wait_ge(ada1_step, 16 * n - 12 + 4 * b)
                    sp.dma_start(ada_first[:, b, :, :], w_tile(ada_w, b, kb * NC + which * D)).then_inc(ada1_in[b], 16)

            first_chunk(0, 0, 0)
            first_chunk(0, 1, 1)
            with sp.Fori(1, 4) as kb:
                first_chunk(kb, 0, 2 * kb)
                first_chunk(kb, 1, 2 * kb + 1)

            def load(w, G, col):
                for b in range(4):
                    if not (isinstance(G, int) and G == 0):
                        sp.wait_ge(split_ready, 8 * G - 8 + 2 * b + 2)
                    sp.dma_start(stage[:, b, :, :], w_tile(w, b, col)).then_inc(loaded[b], 16)

            for s in range(RET_SETS):
                for g, col in enumerate((COL_RQ + s * NC, COL_RK + s * NC, COL_RV + s * 2 * NC,
                                         COL_RV + s * 2 * NC + NC, COL_RG + s * 2 * NC, COL_RG + s * 2 * NC + NC)):
                    load(w_in, 6 * s + g, col)
            with sp.Fori(0, MOBA_SETS) as s:
                for g, col in enumerate((COL_MQ, COL_MK, COL_MV, COL_GB)):
                    load(w_in, G_MOBA + 4 * s + g, col + s * NC)
            for w, G0, col in ((w_in, G_GA, COL_GA), (ret_w_o, G_RETO, 0), (moba_w_o, G_MOBAO, 0), (w_out, G_OUT, 0)):
                with sp.Fori(0, 4) as n:
                    load(w, G0 + n, col + n * NC)
            up = ffn_w_up[0].rearrange("(k p) (c n) -> p k c n", p=P, c=2)
            with sp.Fori(0, UPS) as j:
                for b in range(4):
                    sp.wait_ge(split_ready, 8 * (G_UP + j) - 8 + 2 * b + 2)
                    for half in range(2):
                        sp.dma_start(stage[:, b, :, half * 2 * P:(half + 1) * 2 * P],
                                     up[:, b * KB:(b + 1) * KB, half, bass.ds(j * 2 * P, 2 * P)]).then_inc(loaded[b], 16)
            down = ffn_w_down[0].rearrange("(k p) n -> p k n", p=P)
            with sp.Fori(0, DOWNS) as kb:
                for n in range(4):
                    sp.wait_ge(split_ready, 8 * (G_DOWN + kb) - 8 + 2 * n + 2)
                    sp.dma_start(stage[:, n, :, :],
                                 down[:, bass.ds(kb * KB, KB), n * NC:(n + 1) * NC]).then_inc(loaded[n], 16)
            for t in range(T):
                for n in range(2):
                    sp.wait_ge(out_ready, 2 * t + n + 1)
                    sp.dma_start(out[0, t * P:(t + 1) * P, n * 1024:(n + 1) * 1024],
                                 y_gain[:, t, n * 1024:(n + 1) * 1024]).then_inc(stored, 16)
            sp.wait_ge(stored, 16 * 2 * T)

        @block.gpsimd
        def _(pool):
            pool.memset(ones[:, :], 1.0).then_inc(ones_set, 1)
            bg = ada_w[0].rearrange("(k p) n -> p k n", p=P)

            def chunk(j):
                for q in range(4):
                    if isinstance(j, int) and j == 0 and q < 2:
                        if q == 0:
                            pool.wait_ge(ada1_cols, 8)
                    else:
                        pool.wait_ge(ada_step, 16 * j + 4 * q - 4)
                    pool.dma_start(ada_ring[:, q % 2, :, :],
                                   bg[:, q * KB:(q + 1) * KB, bass.ds(j * ADA_BG + 2 * D, ADA_BG)]
                                   ).then_inc(ada_in[q % 2], 16)
            chunk(0)
            with pool.Fori(1, 4 * D // ADA_BG) as j:
                chunk(j)

        @block.tensor
        def _(pe):
            def product(G, parity, out_before=None, lhs_phase=None, side=None):
                for h in range(HB):
                    if h == 0 and out_before is not None:
                        pe.wait_ge(*out_before)
                    if lhs_phase is not None:
                        pe.wait_ge(lhs_ready, 8 * lhs_phase + h + 1)
                    pe.wait_ge(split_ready, 8 * G + h + 1)
                    for k in range(2):
                        kt = 2 * h + k
                        for t in range(T):
                            acc = ps[:, 2 * parity + t, :]
                            hi = lhs[:, kt, t * P:(t + 1) * P]
                            lo = lhs[:, kt, SEQ + t * P:SEQ + (t + 1) * P]
                            pe.matmul(acc, hi, w_high[:, h % 4, k, :], start=kt == 0, stop=False)
                            pe.matmul(acc, hi, w_low[:, h % 4, k, :], start=False, stop=False)
                            last = pe.matmul(acc, lo, w_high[:, h % 4, k, :], start=False, stop=kt == KT - 1)
                    last.then_inc(used, 1)
                    if side is not None:
                        side(h)

            def turn(bank, tiles):
                for n, tile in enumerate(tiles):
                    last = pe.transpose(ps[:, bank, n * P:(n + 1) * P], tile, ident[:, :])
                return last

            def sum_chunk(j, parity):
                pe.wait_ge(ada_step, 16 * j + 16)
                if not (isinstance(j, int) and j == 0):
                    pe.wait_ge(ada_kept, j)
                for n in range(2):
                    last = pe.matmul(ps[:, 7, n:n + 1], ada_acc[:, parity, n * P:(n + 1) * P], ones[:, 0:1],
                                     start=True, stop=True)
                last.then_inc(ada_summed, 1)

            pe.wait_ge(ident_in, 16)
            pe.wait_ge(rows_in, 16 * 15)
            pe.transpose(ps[:, 4, 0:7 * KT], rows[:, :], ident[0:7 * KT, 0:7 * KT])
            pe.transpose(ps[:, 4, 128:128 + 4 * KT], post_rows[:, :], ident[0:4 * KT, 0:4 * KT])
            for n in range(4):
                last = pe.transpose(ps[:, 5, n * 88:(n + 1) * 88], conv_rows[:, n, :], ident[0:88, 0:88])
            last.then_inc(cols_turned, 1)
            for r in range(2):
                for b in range(4):
                    pair = 4 * r + b
                    if r:
                        pe.wait_ge(xT_ready, b + 1)
                    else:
                        pe.wait_ge(x_scaled, 2)
                    turn(b, [x_sb[:, t, (2 * pair + k) * P:(2 * pair + k + 1) * P]
                             for k in range(2) for t in range(T)]).then_inc(x_turned, 1)
            pe.wait_ge(ones_set, 1)

            def sum_first(n, which):
                pe.wait_ge(ada1_step, 16 * n + 16)
                if isinstance(n, int) and n == 0:
                    pe.wait_ge(cols_ready, 3)
                else:
                    pe.wait_ge(ada1_cols, n)
                for i in range(4):
                    for e in range(2):
                        last = pe.matmul(ps[:, 4, i:i + 1], ada_acc1[:, which, e, i * P:(i + 1) * P], ones[:, 0:1],
                                         start=e == 0, stop=e == 1)
                last.then_inc(ada1_summed, 1)

            sum_first(0, 0)
            sum_first(1, 1)
            with pe.Fori(1, 4) as kb:
                sum_first(2 * kb, 0)
                sum_first(2 * kb + 1, 1)
            def ret_side(G):
                def at(g, h, s):
                    return G == 6 * s + g, h

                def side(h):
                    if h == 1 and G >= 1:
                        sum_chunk(G - 1, (G - 1) % 2)
                    for s in range(RET_SETS):
                        g = G - 6 * s
                        if (g, h) in ((1, 4), (2, 5)):
                            n = 2 * s + g - 1
                            pe.wait_ge(rot_ready, 2 * n + 2)
                            for b in range(2):
                                if n and b == 0:
                                    pe.wait_ge(rqk_ready, n)
                                    if g == 1:
                                        pe.wait_ge(ret_kept, 2 * s)
                                last = turn(4 + b, [rot[:, t, (2 * b + hd) * P:(2 * b + hd + 1) * P]
                                                    for hd in range(2) for t in range(T)])
                            last.then_inc(rqk_turned, 1)
                        if (g, h) == (3, 0):
                            pe.wait_ge(rqk_ready, 2 * s + 2)
                            for hd in range(SETH):
                                pe.matmul(ps[:, 5 + hd // 2, hd % 2 * SEQ:(hd % 2 + 1) * SEQ], kT_ret[:, hd, 0:P],
                                          qT_ret[:, hd, :], start=True, stop=True)
                                last = pe.matmul(ps[:, 4, hd * P:(hd + 1) * P], kT_ret[:, hd, P:SEQ],
                                                 qT_ret[:, hd, P:SEQ], start=True, stop=True)
                            last.then_inc(ret_scored, 1)
                        if (g, h) in ((3, 6), (4, 3)):
                            n = 2 * s + g - 3
                            if g == 3:
                                pe.wait_ge(ret_decayed, 2 * s + 2)
                            else:
                                pe.wait_ge(gn_ready, 4 * n)
                            pe.wait_ge(rv_ready, 2 * n + 2)
                            for i in range(2):
                                hd = 2 * (g - 3) + i
                                v0, v1 = (v_ret[:, t, hd * RET_DV:(hd + 1) * RET_DV] for t in range(T))
                                pe.matmul(ps[:, 4 + i, 0:RET_DV], sT0[:, hd, 0:P], v0, start=True, stop=True)
                                pe.matmul(ps[:, 4 + i, RET_DV:2 * RET_DV], sT0[:, hd, P:SEQ], v0, start=True, stop=False)
                                last = pe.matmul(ps[:, 4 + i, RET_DV:2 * RET_DV], sT1[:, hd, :], v1,
                                                 start=False, stop=True)
                            last.then_inc(ret_summed, 1)
                        if (g, h) in ((5, 2), (6, 2)):
                            n = 2 * s + g - 5
                            pe.wait_ge(ret_gated, n + 1)
                            if g == 5:
                                pe.wait_ge(gn_ready, 8 * s + 8)
                            else:
                                pe.wait_ge(ret_kept, n)
                            for b in range(2):
                                last = turn(4 + b, [o_ret[:, t, (g - 5) * NC + (2 * b + e) * P:(g - 5) * NC + (2 * b + e + 1) * P]
                                                    for e in range(2) for t in range(T)])
                            last.then_inc(ret_turned, 1)
                return side

            for G in range(G_MOBA):
                product(G, G % 2, out_of_psum(G - 2), 0 if G == 0 else None, ret_side(G))

            def moba_set(s, first):
                def side_of(g):
                    ret = ret_side(G_MOBA) if first and g == 0 else None

                    def side(h):
                        if ret is not None:
                            ret(h)
                        elif h == 1:
                            sum_chunk(G_MOBA + 4 * s + g - 1, (g + 1) % 2)
                        if (g, h) in ((1, 1), (2, 1)):
                            if g == 1 and not first:
                                pe.wait_ge(att_kept, s)
                            if g == 1 and first:
                                pe.wait_ge(ret_kept, 2 * RET_SETS)
                            if g == 2:
                                pe.wait_ge(mqk_ready, 2 * s + 1)
                            pe.wait_ge(mqk_nat, 4 * s + 2 * g)
                            for b in range(2):
                                last = turn(4 + b, [qk_nat[:, t, (2 * b + hd) * P:(2 * b + hd + 1) * P]
                                                    for hd in range(2) for t in range(T)])
                            last.then_inc(mqk_turned, 1)
                        if (g, h) == (2, 4):
                            pe.wait_ge(mqk_ready, 2 * s + 2)
                            for hd in range(SETH):
                                pe.matmul(ps[:, 4, hd * P:(hd + 1) * P], qT[:, hd, 0:P], kT[:, hd, 0:P],
                                          start=True, stop=True)
                                last = pe.matmul(ps[:, 5 + hd // 2, hd % 2 * SEQ:(hd % 2 + 1) * SEQ], qT[:, hd, P:SEQ],
                                                 kT[:, hd, :], start=True, stop=True)
                            last.then_inc(scored, 1)
                        if (g, h) == (3, 4):
                            pe.wait_ge(probs_ready, 2 * s + 2)
                            turn(4, [p0[:, hd, :] for hd in range(SETH)])
                            for b in range(2):
                                last = turn(5 + b, [p1[:, 2 * b + hd, kk * P:(kk + 1) * P]
                                                    for hd in range(2) for kk in range(2)])
                            last.then_inc(probs_turned, 1)
                        if (g, h) == (3, 7):
                            pe.wait_ge(probsT_ready, 3 * s + 3)
                            pe.wait_ge(mv_ready, 2 * s + 2)
                            for hd in range(SETH):
                                o = ps[:, 4 + hd // 2, hd % 2 * SEQ:(hd % 2 + 1) * SEQ]
                                pe.matmul(o, v_moba[:, 0, hd * P:(hd + 1) * P], pTa[:, hd, :], start=True, stop=False)
                                last = pe.matmul(o[:, P:SEQ], v_moba[:, 1, hd * P:(hd + 1) * P], pTb[:, hd, :],
                                                 start=False, stop=True)
                            last.then_inc(attended, 1)
                    return side
                for g in range(4):
                    if g >= 2:
                        before = moba_out_of_psum(s, g - 2)
                    else:
                        before = out_of_psum(G_MOBA + g - 2) if first else moba_out_of_psum(s - 1, g + 2)
                    product(G_MOBA + 4 * s + g, g % 2, before, None, side_of(g))

            moba_set(0, True)
            with pe.Fori(1, MOBA_SETS) as s:
                moba_set(s, False)

            def spread_gain(n):
                pe.wait_ge(gain_diag, 4 * n + 4)
                if n:
                    pe.wait_ge(gain_ready, n)
                for i in range(4):
                    last = pe.matmul(ps[:, 6, i * P:(i + 1) * P], ones[:, :], diag1[:, (4 * (n % 2) + i) * P:(4 * (n % 2) + i + 1) * P], start=True, stop=True)
                last.then_inc(gain_spread, 1)

            for G in range(G_GA, G_UP):
                def side(h):
                    if h == 1 and G <= G_RETO:
                        sum_chunk(G - 1, (G - 1) % 2)
                    if G > G_MOBAO and G <= G_OUT and h == 1:
                        n = G - 1 - G_MOBAO
                        pe.wait_ge(gated, 8 + 3 * (n + 1))
                        if n == 0:
                            pe.wait_ge(att_kept, MOBA_SETS)
                        else:
                            pe.wait_ge(merge_kept, n)
                        for b in range(2):
                            last = turn(4 + b, [gate_a[:, t, (4 * n + 2 * b + e) * P:(4 * n + 2 * b + e + 1) * P]
                                                for e in range(2) for t in range(T)])
                        last.then_inc(merge_turned, 1)
                    if G_MOBAO <= G < G_OUT and h == 4:
                        spread_gain(G - G_MOBAO)
                phase = (G - G_RETO) // 4 + 1 if G >= G_RETO and (G - G_RETO) % 4 == 0 else None
                product(G, G % 2, out_of_psum(G - 2), phase, side)

            for t in range(T):
                pe.wait_ge(x2_scaled, t + 1)
                for kt in range(KT):
                    if t == 0 and kt == 0:
                        pe.wait_ge(y_gained, 8)
                        pe.wait_ge(merge_kept, 4)
                    last = pe.transpose(ps[:, kt // 2, (kt % 2) * SEQ + t * P:(kt % 2) * SEQ + (t + 1) * P],
                                        y_gain[:, t, kt * P:(kt + 1) * P], ident[:, :])
                    if t == T - 1 and kt % 2 == 1:
                        last.then_inc(x2_turned, 1)

            def up_product(j, parity, first):
                G = G_UP + j
                for h in range(HB):
                    if h == 0:
                        if first and parity == 0:
                            pe.wait_ge(u2_ready, KT // 2)
                        elif first:
                            pe.wait_ge(gain_ready, 5)
                        else:
                            pe.wait_ge(up_sum, j - 1)
                    if first and parity == 0:
                        pe.wait_ge(lhs_ready, 8 * 4 + h + 1)
                    pe.wait_ge(split_ready, 8 * G + h + 1)
                    for k in range(2):
                        kt = 2 * h + k
                        for ct in range(4):
                            pe.matmul(ps[:, 4 * parity + ct, :], w_high[:, h % 4, k, ct * P:(ct + 1) * P], lhs[:, kt, :],
                                      start=kt == 0, stop=False)
                            last = pe.matmul(ps[:, 4 * parity + ct, 0:SEQ], w_low[:, h % 4, k, ct * P:(ct + 1) * P],
                                             lhs[:, kt, 0:SEQ], start=False, stop=kt == KT - 1)
                    last.then_inc(used, 1)
                    if first and parity == 0 and h == 5:
                        pe.wait_ge(u2_ready, KT)
                        pe.wait_ge(gain_diag, 2 * KT)
                        for i in range(KT):
                            last = pe.matmul(ps[:, 4 + i // 4, i % 4 * P:(i % 4 + 1) * P], ones[:, :],
                                             diag2[:, i * P:(i + 1) * P], start=True, stop=True)
                        last.then_inc(gain_spread, 1)

            up_product(0, 0, True)
            up_product(1, 1, True)
            with pe.Fori(1, UPS // 2) as i:
                up_product(2 * i, 0, False)
                up_product(2 * i + 1, 1, False)

            def down_step(kb, parity, first=False, final=False):
                G = G_DOWN + kb
                for h in range(HB):
                    n = h // 2
                    if h < 2:
                        pe.wait_ge(g_split, 2 * kb + h + 1)
                    if first and h == 0:
                        pe.wait_ge(up_sum, UPS - 1)
                    if first and h == 4:
                        pe.wait_ge(up_sum, UPS)
                    pe.wait_ge(split_ready, 8 * G + h + 1)
                    for k in range(2):
                        kk = 2 * (h % 2) + k
                        for t in range(T):
                            acc = ps[:, 2 * n + t, :]
                            hi = g_lhs[:, parity, kk, t * P:(t + 1) * P]
                            lo = g_lhs[:, parity, kk, SEQ + t * P:SEQ + (t + 1) * P]
                            pe.matmul(acc, hi, w_high[:, h % 4, k, :], start=first and kk == 0, stop=False)
                            pe.matmul(acc, hi, w_low[:, h % 4, k, :], start=False, stop=False)
                            last = pe.matmul(acc, lo, w_high[:, h % 4, k, :], start=False, stop=final and kk == 3)
                    last.then_inc(used, 1)

            down_step(0, 0, first=True)
            with pe.Fori(0, (DOWNS - 3) // 2) as i:
                down_step(2 * i + 1, 1)
                down_step(2 * i + 2, 0)
            down_step(DOWNS - 2, 1)
            down_step(DOWNS - 1, 0, final=True)

        @block.scalar
        def _(act):
            def group(G, side=None, loads=None):
                for h in range(HB):
                    if h % 2 == 0:
                        act.wait_ge(loaded[h // 2], 16 * (G + 1 if loads is None else loads))
                    wait(act, used, 8 * G + h - 3)
                    act.activation(w_high[:, h % 4, :, :], stage[:, h // 2, 2 * (h % 2):2 * (h % 2) + 2, :],
                                   ACT.Copy).then_inc(high_ready, 1)
                    if side is not None:
                        side(h)

            def lhs_pair(phase, i, src, G_before):
                wait(act, used, 8 * G_before + i + 1)
                act.activation(lhs[:, 2 * i:2 * i + 2, 0:SEQ], src[:, 2 * i:2 * i + 2, :], ACT.Copy
                               ).then_inc(lhs_high, 1)

            def root_of_norm(k):
                act.wait_ge(norm_mean, k + 1)
                act.activation(rstd[:, :], rstd[:, :], ACT.Sqrt).then_inc(norm_root, 1)

            act.dma_start(ident[:, :], identity[:, :]).then_inc(ident_in, 16)
            act.dma_start(cos2[:, :, :], rope_cos[:, :, :]).then_inc(consts_in, 16)
            act.dma_start(sin2[:, :, :], rope_sin[:, :, :]).then_inc(consts_in, 16)
            act.dma_start(mask[:, :], causal[:, :]).then_inc(consts_in, 16)
            act.wait_ge(cols_turned, 1)
            act.activation(cols[:, :], ps[:, 4, 0:7 * KT], ACT.Copy).then_inc(cols_ready, 1)
            act.activation(post_cols[:, :], ps[:, 4, 128:128 + 4 * KT], ACT.Copy).then_inc(cols_ready, 1)
            act.activation(c_act[:, :], ps[:, 4, 0:KT], ACT.Silu).then_inc(cols_ready, 1)
            act.activation(conv_cols[:, :, :], ps[:, 5, 0:352].rearrange("p (n k) -> p n k", n=4), ACT.Copy
                           ).then_inc(cols_ready, 1)
            act.dma_start(decay[:, :, :], decay_dram[:, :, :]).then_inc(decay_in, 16)
            junk = src_b[:, 0:8, :].rearrange("p k n -> p (k n)")
            for t in range(T):
                act.wait_ge(x_in[t], 16)
                if t:
                    act.wait_ge(squared, t)
                act.activation(junk, x_sb[:, t, :], ACT.Square, accum_out=squares[:, t, 0:1]).then_inc(squared, 1)
            root_of_norm(0)
            act.wait_ge(norm_inv, 1)
            for t in range(T):
                act.activation(x_sb[:, t, :], x_sb[:, t, :], ACT.Copy, scale=rstd[:, t:t + 1]).then_inc(x_scaled, 1)
            for i in range(KT // 2):
                act.wait_ge(x_turned, i + 1)
                act.activation(src_a[:, 2 * i:2 * i + 2, :], ps[:, i % 4, :].rearrange("p (k n) -> p k n", k=2),
                               ACT.Copy).then_inc(xT_ready, 1)

            def ret_side(G):
                def side(h):
                    if G == 0:
                        act.wait_ge(u_ready, 2 * h + 2)
                        lhs_pair(0, h, src_b, -1)
                    for s in range(RET_SETS):
                        g = G - 6 * s
                        if (g, h) in ((2, 0), (3, 1)):
                            n = 2 * s + g - 2
                            act.wait_ge(rqk_turned, n + 1)
                            wait(act, ret_scored, s)
                            act.activation((qT_ret, kT_ret)[g - 2][:, :, :],
                                           ps[:, 4:6, :].rearrange("p b (h n) -> p (b h) n", h=2),
                                           ACT.Copy).then_inc(rqk_ready, 1)
                        if h == 3 and g in (3, 4):
                            act.wait_ge(used, 8 * G)
                            wait(act, ret_summed, 2 * s)
                            for t in range(T):
                                act.activation(v_ret[:, t, (g - 3) * NC:(g - 2) * NC], ps[:, 2 * ((G - 1) % 2) + t, :],
                                               ACT.Copy).then_inc(rv_ready, 1)
                        if (g, h) in ((4, 2), (4, 7)):
                            n = 2 * s + h // 7
                            act.wait_ge(gn_var, n + 1)
                            act.activation(inv_std[:, :], inv_std[:, :], ACT.Sqrt).then_inc(gn_root, 1)
                        if h == 3 and g in (5, 6):
                            n = 2 * s + g - 5
                            act.wait_ge(used, 8 * G)
                            wait(act, ret_gated, n)
                            act.activation(gate_r[:, :, :], ps[:, 2 * ((G - 1) % 2):2 * ((G - 1) % 2) + 2, :],
                                           ACT.Silu).then_inc(rg_ready, 1)
                        if (g, h) in ((5, 6), (6, 6)):
                            n = 2 * s + g - 5
                            act.wait_ge(ret_turned, n + 1)
                            act.activation(src_a[:, 4 * n:4 * n + 4, :],
                                           ps[:, 4:6, :].rearrange("p b (k n) -> p (b k) n", k=2),
                                           ACT.Copy).then_inc(ret_kept, 1)
                return side

            for G in range(G_MOBA):
                group(G, ret_side(G))

            def keep_attended(s):
                act.wait_ge(attended, s + 1)
                act.activation(src_b[:, bass.ds(SETH * s, SETH), :], ps[:, 4:6, :].rearrange("p b (h n) -> p (b h) n", h=2),
                               ACT.Copy).then_inc(att_kept, 1)

            def keep_gate(gate, G_next, parity, col):
                act.wait_ge(used, 8 * G_next)
                for t in range(T):
                    act.activation(gate[:, t, bass.ds(col, NC)], ps[:, 2 * parity + t, :], ACT.Sigmoid
                                   ).then_inc(gate_ready, 1)

            def moba_set(s, first):
                def side_of(g):
                    ret = ret_side(G_MOBA) if first and g == 0 else None
                    G = G_MOBA + 4 * s + g

                    def side(h):
                        if ret is not None:
                            ret(h)
                        if (g, h) == (0, 3) and not first:
                            keep_attended(s - 1)
                            keep_gate(gate_b, G, 1, (s - 1) * NC)
                        if h == 3 and g in (1, 2):
                            act.wait_ge(used, 8 * G)
                            if not (first and g == 1):
                                act.wait_ge(mqk_turned, 2 * s + g - 1)
                            for t in range(T):
                                act.activation(qk_nat[:, t, :], ps[:, 2 * (1 - g % 2) + t, :], ACT.Copy
                                               ).then_inc(mqk_nat, 1)
                        if h == 5 and g in (1, 2):
                            act.wait_ge(mqk_turned, 2 * s + g)
                            if not first:
                                act.wait_ge(scored, s)
                            act.activation((qT, kT)[g - 1][:, :, :], ps[:, 4:6, :].rearrange("p b (h n) -> p (b h) n", h=2),
                                           ACT.Copy).then_inc(mqk_ready, 1)
                        if (g, h) == (3, 2):
                            act.wait_ge(neg_ready, s + 1)
                            for hd in range(SETH):
                                act.activation(p0[:, hd, :], p0[:, hd, :], ACT.Exp, bias=neg_max[:, hd:hd + 1],
                                               accum_out=row_sum[:, hd:hd + 1]).then_inc(exp_ready, 1)
                            for hd in range(SETH):
                                n = SETH + hd
                                act.activation(p1[:, hd, :], p1[:, hd, :], ACT.Exp, bias=neg_max[:, n:n + 1],
                                               accum_out=row_sum[:, n:n + 1]).then_inc(exp_ready, 1)
                        if (g, h) == (3, 3):
                            act.wait_ge(used, 8 * G)
                            if not first:
                                act.wait_ge(attended, s)
                            for t in range(T):
                                act.activation(v_moba[:, t, :], ps[:, t, :], ACT.Copy).then_inc(mv_ready, 1)
                        if (g, h) == (3, 6):
                            act.wait_ge(probs_turned, s + 1)
                            if not first:
                                act.wait_ge(attended, s)
                            act.activation(pTa[:, :, 0:P], ps[:, 4, :].rearrange("p (h n) -> p h n", h=SETH),
                                           ACT.Copy).then_inc(probsT_ready, 1)
                            act.activation(pTa[:, :, P:SEQ], ps[:, 5:7, :].rearrange("p b (h n) -> p (b h) n", h=2)[:, :, 0:P],
                                           ACT.Copy).then_inc(probsT_ready, 1)
                            act.activation(pTb[:, :, :], ps[:, 5:7, :].rearrange("p b (h n) -> p (b h) n", h=2)[:, :, P:SEQ],
                                           ACT.Copy).then_inc(probsT_ready, 1)
                    return side
                for g in range(4):
                    group(G_MOBA + 4 * s + g, side_of(g))

            moba_set(0, True)
            with act.Fori(1, MOBA_SETS) as s:
                moba_set(s, False)

            def square_y(n, parity):
                act.wait_ge(used, 8 * (G_OUT + n + 1))
                for t in range(T):
                    wait(act, y_squared, 2 * n + t)
                    act.activation(gT[:, 40:42, :].rearrange("p k n -> p (k n)"), ps[:, 2 * parity + t, :], ACT.Square,
                                   accum_out=squares[:, t, n:n + 1]).then_inc(y_squared, 1)

            def source_kept(phase, i):
                return ((ret_kept, 2 * RET_SETS), (att_kept, MOBA_SETS), (merge_kept, i // 2 + 1))[phase - 1]

            for G in range(G_GA, G_UP):
                phase, n = divmod(G - G_GA, 4)

                def side(h):
                    if G == G_GA and h == 3:
                        keep_attended(MOBA_SETS - 1)
                        keep_gate(gate_b, G, 1, (MOBA_SETS - 1) * NC)
                    if G_GA < G <= G_RETO and h == 3:
                        keep_gate(gate_a, G, (G - 1) % 2, (G - 1 - G_GA) * NC)
                    if n == 3 and phase < 3 and h >= 4:
                        act.wait_ge(*source_kept(phase + 1, h - 4))
                        lhs_pair(phase + 1, h - 4, (src_a, src_b, src_a)[phase], G)
                    if n == 0 and phase > 0:
                        i = 4 + h if h < 2 or (phase < 3 and h < 4) else h if phase == 3 and h >= 6 else None
                        if i is not None:
                            act.wait_ge(*source_kept(phase, i))
                            lhs_pair(phase, i, (src_a, src_b, src_a)[phase - 1], G - 1)
                    if G_MOBAO < G <= G_OUT and h == 5:
                        k = G - 1 - G_MOBAO
                        act.wait_ge(merge_turned, k + 1)
                        act.activation(src_a[:, 4 * k:4 * k + 4, :], ps[:, 4:6, :].rearrange("p b (k n) -> p (b k) n", k=2),
                                       ACT.Copy).then_inc(merge_kept, 1)
                    if G_MOBAO < G <= G_OUT and h == 0:
                        k = G - 1 - G_MOBAO
                        act.wait_ge(gain_spread, k + 1)
                        act.activation(gain_b[:, k * NC:(k + 1) * NC], ps[:, 6, :], ACT.Copy).then_inc(gain_ready, 1)
                    if G == G_OUT and h == 5:
                        act.wait_ge(gated, 8 + 12)
                        for t in range(T):
                            act.dma_start(x_sb[:, t, :], x[0, t * P:(t + 1) * P, :]).then_inc(x_back, 16)
                    if G > G_OUT and h == 3:
                        square_y(G - 1 - G_OUT, (G - 1) % 2)
                group(G, side)

            def up_side(j, par_before):
                def side(h):
                    if h == 3:
                        act.wait_ge(used, 8 * (G_UP + j))
                        wait(act, up_sum, j - 1)
                        act.activation(h_low[:, :, :], ps[:, 4 * par_before:4 * par_before + 4, SEQ:2 * SEQ],
                                       ACT.Copy).then_inc(up_low, 1)
                    if h == 7:
                        act.wait_ge(conv_step, 12 * j)
                        wait(act, g_ready, j - 1)
                        act.activation(a_act[:, :, :], h_conv[:, 0:2, :], ACT.Silu).then_inc(a_ready, 1)
                return side

            def first_up_side(h):
                if h == 3:
                    square_y(3, 1)
                    root_of_norm(1)
                    spare = gT[:, 16:24, :].rearrange("p k n -> p (k n)")
                    for t in range(T):
                        act.wait_ge(x2_ready, t + 1)
                        if t:
                            act.wait_ge(x2_squared, 1)
                        act.activation(spare, x_sb[:, t, :], ACT.Square, accum_out=squares[:, t, 0:1]
                                       ).then_inc(x2_squared, 1)
                    root_of_norm(2)
                    for i in range(4):
                        act.wait_ge(u2_ready, 2 * i + 2)
                        lhs_pair(4, i, gT, G_UP - 1)
                if h > 3:
                    act.wait_ge(u2_ready, 2 * h + 2)
                    lhs_pair(4, h, gT, G_UP - 1)

            def second_up_side(h):
                if h == 1:
                    act.wait_ge(gain_spread, 5)
                    act.activation(gain_b[:, :].rearrange("p (b n) -> p b n", b=4), ps[:, 4:8, :], ACT.Copy
                                   ).then_inc(gain_ready, 1)
                up_side(1, 0)(h)

            def up_loads(j):
                return G_UP + 2 * j + 2
            group(G_UP, first_up_side, up_loads(0))
            group(G_UP + 1, second_up_side, up_loads(1))
            with act.Fori(1, UPS // 2) as i:
                group(G_UP + 2 * i, up_side(2 * i, 1), up_loads(2 * i))
                group(G_UP + 2 * i + 1, up_side(2 * i + 1, 0), up_loads(2 * i + 1))

            def g_part(kb, i, parity):
                act.wait_ge(g_ready, 2 * kb + i + 1)
                wait(act, used, 8 * (G_DOWN + kb - 1))
                act.activation(g_lhs[:, parity, 2 * i:2 * i + 2, 0:SEQ], gT[:, bass.ds(KB * kb + 2 * i, 2), :], ACT.Copy
                               ).then_inc(g_high, 1)

            def down_side(kb, parity, first=False):
                def side(h):
                    if first and h < 2:
                        g_part(0, h, 0)
                    if first:
                        up_side(UPS, 1)(h)
                    if h in (4, 5):
                        g_part(kb + 1, h - 4, 1 - parity)
                return side

            def down_loads(kb):
                return G_DOWN + UPS + kb + 1
            group(G_DOWN, down_side(0, 0, True), down_loads(0))
            with act.Fori(0, (DOWNS - 3) // 2) as i:
                group(G_DOWN + 2 * i + 1, down_side(2 * i + 1, 1), down_loads(2 * i + 1))
                group(G_DOWN + 2 * i + 2, down_side(2 * i + 2, 0), down_loads(2 * i + 2))
            group(G_DOWN + DOWNS - 2, down_side(DOWNS - 2, 1), down_loads(DOWNS - 2))
            group(G_DOWN + DOWNS - 1, None, down_loads(DOWNS - 1))
            for n in range(4):
                act.wait_ge(used, 8 * (G_DOWN + DOWNS - 1) + 2 * n + 2)
                for t in range(T):
                    wait(act, y2_squared, 2 * n + t)
                    act.activation(gT[:, 0:2, :].rearrange("p k n -> p (k n)"), ps[:, 2 * n + t, :], ACT.Square, accum_out=squares[:, t, n:n + 1]
                                   ).then_inc(y2_squared, 1)
            root_of_norm(3)

        @block.vector
        def _(dve):
            def low_part(G, h):
                dve.wait_ge(high_ready, 8 * G + h + 1)
                dve.tensor_tensor(w_low[:, h % 4, :, :], stage[:, h // 2, 2 * (h % 2):2 * (h % 2) + 2, :],
                                  w_high[:, h % 4, :, :].bitcast(F32), ALU.subtract).then_inc(split_ready, 1)

            def group(G, side=None, ada=None):
                for h in range(HB):
                    if ada is not None:
                        ada_step_of(*ada, 2 * h)
                    low_part(G, h)
                    if ada is not None:
                        ada_step_of(*ada, 2 * h + 1)
                    if side is not None:
                        side(h)

            def ada_step_of(j, parity, i):
                b = i // KB
                if i % KB == 0:
                    dve.wait_ge(ada_in[b % 2], 16 * (2 * j + b // 2 + 1))
                block_, acc = ada_ring[:, b % 2, i % KB, :], ada_acc[:, parity, :]
                if i == 0:
                    if not (isinstance(j, int) and j < 2):
                        dve.wait_ge(ada_summed, j - 1)
                    op = dve.tensor_scalar(acc, block_, c_act[:, 0:1], None, ALU.mult)
                else:
                    dve.wait_ge(ada_step, 16 * j + i)
                    op = dve.scalar_tensor_tensor(out=acc, in0=block_, scalar=c_act[:, i:i + 1], in1=acc,
                                                  op0=ALU.mult, op1=ALU.add)
                op.then_inc(ada_step, 1)

            def keep_chunk(j):
                dve.wait_ge(ada_summed, j + 1)
                dve.tensor_copy(ada_cols[:, bass.ds(2 * j, 2)], ps[:, 7, 0:2]).then_inc(ada_kept, 1)

            def lhs_pair(phase, i, src):
                dve.wait_ge(lhs_high, 8 * phase + i + 1)
                dve.tensor_tensor(lhs[:, 2 * i:2 * i + 2, SEQ:2 * SEQ], src[:, 2 * i:2 * i + 2, :],
                                  lhs[:, 2 * i:2 * i + 2, 0:SEQ].bitcast(F32), ALU.subtract).then_inc(lhs_ready, 1)

            def rstd_of(k, parts):
                src = squares[:, :, 0]
                if parts > 1:
                    dve.tensor_reduce(mean_sq[:, :], squares[:, :, 0:parts], AX.X, ALU.add).then_inc(norm_sum, 1)
                    dve.wait_ge(norm_sum, 1 if k == 1 else 2)
                    src = mean_sq[:, :]
                dve.tensor_scalar(rstd[:, :], src, 1.0 / D, NORM_EPS, ALU.mult, ALU.add).then_inc(norm_mean, 1)
                dve.wait_ge(norm_root, k + 1)
                dve.reciprocal(rstd[:, :], rstd[:, :]).then_inc(norm_inv, 1)
                dve.wait_ge(norm_inv, k + 1)

            dve.wait_ge(squared, 2)
            rstd_of(0, 1)
            dve.wait_ge(cols_ready, 4)

            def first_chunk(kb, which, n):
                for i in range(KT):
                    if i % KB == 0:
                        dve.wait_ge(ada1_in[i // KB], 16 * (n + 1))
                    block_, acc = ada_first[:, i // KB, i % KB, :], ada_acc1[:, which, i % 2, :]
                    if i < 2:
                        if not (isinstance(n, int) and n < 2):
                            dve.wait_ge(ada1_summed, n - 1)
                        op = dve.tensor_scalar(acc, block_, c_act[:, i:i + 1], None, ALU.mult)
                    else:
                        dve.wait_ge(ada1_step, 16 * n + i - 1)
                        op = dve.scalar_tensor_tensor(out=acc, in0=block_, scalar=c_act[:, i:i + 1], in1=acc,
                                                      op0=ALU.mult, op1=ALU.add)
                    op.then_inc(ada1_step, 1)
                dve.wait_ge(ada1_summed, n + 1)
                here = bass.ds(KB * kb, KB)
                if which == 0:
                    dve.tensor_tensor(shift1[:, here], ps[:, 4, 0:KB], cols[:, bass.ds(3 * KT + KB * kb, KB)], ALU.add
                                      ).then_inc(ada1_cols, 1)
                else:
                    dve.scalar_tensor_tensor(out=scale1[:, here], in0=ps[:, 4, 0:KB], scalar=1.0,
                                             in1=cols[:, bass.ds(4 * KT + KB * kb, KB)], op0=ALU.add, op1=ALU.add
                                             ).then_inc(ada1_cols, 1)

            first_chunk(0, 0, 0)
            first_chunk(0, 1, 1)
            with dve.Fori(1, 4) as kb:
                first_chunk(kb, 0, 2 * kb)
                first_chunk(kb, 1, 2 * kb + 1)
            dve.wait_ge(ada1_cols, 8)
            dve.tensor_tensor(scale1[:, :], scale1[:, :], cols[:, KT:2 * KT], ALU.mult).then_inc(mod1, 1)
            dve.wait_ge(mod1, 1)
            dve.wait_ge(xT_ready, 8)
            dve.wait_ge(consts_in, 48)

            def rotate(n, t, G):
                i = 2 * n + t
                src = ps[:, 2 * (G % 2) + t, :].rearrange("p (h d) -> p h d", h=SETH)
                r_cos, r_sin = (r[:, :].rearrange("p (h d) -> p h d", h=SETH) for r in (rot_cos, rot_sin))
                half = RET_DK // 2
                dve.wait_ge(used, 8 * G + 8)
                wait(dve, rot_ready, i)
                dve.tensor_tensor(r_cos, src, cos2[:, t, :].unsqueeze(1).broadcast_to([P, SETH, P]), ALU.mult
                                  ).then_inc(rot_terms, 1)
                for a, b in ((0, half), (half, 0)):
                    dve.tensor_tensor(r_sin[:, :, a:a + half], src[:, :, b:b + half],
                                      sin2[:, t, a:a + half].unsqueeze(1).broadcast_to([P, SETH, half]), ALU.mult
                                      ).then_inc(rot_terms, 1)
                dve.wait_ge(rot_terms, 3 * i + 3)
                wait(dve, rqk_turned, n)
                dve.tensor_tensor(rot[:, t, :], rot_cos[:, :], rot_sin[:, :], ALU.add).then_inc(rot_ready, 1)

            def head_outs():
                return [(hd, t, ps[:, 4 + hd, t * RET_DV:(t + 1) * RET_DV]) for hd in range(2) for t in range(T)]

            def norm_heads(s, i):
                n = 2 * s + i
                dve.wait_ge(ret_summed, n + 1)
                outs = head_outs()
                for k, (hd, t, o) in enumerate(outs):
                    dve.bn_stats(stats[:, k, :], o).then_inc(gn_stats, 1)
                for k in range(4):
                    dve.wait_ge(gn_stats, 4 * n + k + 1)
                    dve.bn_aggr(moments[:, k, :], stats[:, k, :]).then_inc(gn_moments, 1)
                dve.wait_ge(gn_moments, 4 * n + 4)
                dve.tensor_scalar(inv_std[:, :], moments[:, :, 1], GN_EPS, None, ALU.add).then_inc(gn_var, 1)

            def scale_heads(s, i):
                n = 2 * s + i
                outs = head_outs()
                dve.wait_ge(gn_root, n + 1)
                dve.reciprocal(inv_std[:, :], inv_std[:, :]).then_inc(gn_inv, 1)
                dve.wait_ge(gn_inv, n + 1)
                wait(dve, ret_turned, n - 1)
                for k, (hd, t, o) in enumerate(outs):
                    at = (2 * i + hd) * RET_DV
                    dve.tensor_scalar(o_ret[:, t, at:at + RET_DV], o, moments[:, k, 0:1], inv_std[:, k:k + 1],
                                      ALU.subtract, ALU.mult).then_inc(gn_ready, 1)

            def ret_side(G):
                def side(h):
                    if G == 0:
                        for kt in (2 * h, 2 * h + 1):
                            dve.tensor_scalar(src_b[:, kt, :], src_a[:, kt, :], scale1[:, kt:kt + 1],
                                              shift1[:, kt:kt + 1], ALU.mult, ALU.add).then_inc(u_ready, 1)
                        lhs_pair(0, h, src_b)
                    if h == 6 and G >= 1:
                        keep_chunk(G - 1)
                    for s in range(RET_SETS):
                        g = G - 6 * s
                        if g in (1, 2) and h in (3, 4):
                            rotate(2 * s + g - 1, h - 3, G - 1)
                        if (g, h) == (3, 4):
                            dve.wait_ge(ret_scored, s + 1)
                            wait(dve, ret_summed, 2 * s)
                            if s == 0:
                                dve.wait_ge(decay_in, 16)
                            dec = decay[:, SETH * s:SETH * s + SETH, :]
                            dve.tensor_tensor(sT0[:, :, :], ps[:, 5:7, :].rearrange("p b (h n) -> p (b h) n", h=2), dec,
                                              ALU.mult).then_inc(ret_decayed, 1)
                            dve.tensor_tensor(sT1[:, :, :], ps[:, 4, :].rearrange("p (h n) -> p h n", h=SETH),
                                              dec[:, :, 0:P], ALU.mult).then_inc(ret_decayed, 1)
                        if (g, h) == (4, 2):
                            norm_heads(s, 0)
                        if (g, h) == (4, 3):
                            scale_heads(s, 0)
                        if (g, h) == (4, 7):
                            norm_heads(s, 1)
                        if (g, h) == (5, 0):
                            scale_heads(s, 1)
                        if (g, h) in ((5, 4), (6, 4)):
                            n = 2 * s + g - 5
                            dve.wait_ge(rg_ready, n + 1)
                            dve.wait_ge(gn_ready, 4 * n + 4)
                            o = o_ret[:, :, (g - 5) * NC:(g - 4) * NC]
                            dve.tensor_tensor(o, o, gate_r[:, :, :], ALU.mult).then_inc(ret_gated, 1)
                return side

            for G in range(G_MOBA):
                group(G, ret_side(G), (G, G % 2))

            def moba_set(s, first):
                def side_of(g):
                    ret = ret_side(G_MOBA) if first and g == 0 else None

                    def side(h):
                        if ret is not None:
                            ret(h)
                        elif h == 6:
                            keep_chunk(G_MOBA + 4 * s + g - 1)
                        if (g, h) == (3, 0):
                            dve.wait_ge(scored, s + 1)
                            if not first:
                                dve.wait_ge(probs_turned, s)
                            scale = 1.0 / math.sqrt(MOBA_HD)
                            dve.scalar_tensor_tensor(
                                out=p0[:, :, :], in0=ps[:, 4, :].rearrange("p (h n) -> p h n", h=SETH), scalar=scale,
                                in1=mask[:, 0:P].unsqueeze(1).broadcast_to([P, SETH, P]),
                                op0=ALU.mult, op1=ALU.add).then_inc(masked, 1)
                            dve.scalar_tensor_tensor(
                                out=p1[:, :, :], in0=ps[:, 5:7, :].rearrange("p b (h n) -> p (b h) n", h=2), scalar=scale,
                                in1=mask[:, P:3 * P].unsqueeze(1).broadcast_to([P, SETH, SEQ]),
                                op0=ALU.mult, op1=ALU.add).then_inc(masked, 1)
                        if (g, h) == (3, 1):
                            dve.wait_ge(masked, 2 * s + 2)
                            dve.tensor_reduce(row_max[:, 0:SETH], p0[:, :, :], AX.X, ALU.max).then_inc(maxed, 1)
                            dve.tensor_reduce(row_max[:, SETH:2 * SETH], p1[:, :, :], AX.X, ALU.max).then_inc(maxed, 1)
                            dve.wait_ge(maxed, 2 * s + 2)
                            dve.tensor_scalar(neg_max[:, :], row_max[:, :], -1.0, None, ALU.mult).then_inc(neg_ready, 1)
                        if (g, h) == (3, 4):
                            dve.wait_ge(exp_ready, 8 * s + 8)
                            dve.reciprocal(inv_sum[:, :], row_sum[:, :]).then_inc(inv_ready, 1)
                            dve.wait_ge(inv_ready, s + 1)
                            dve.tensor_tensor(p0[:, :, :], p0[:, :, :],
                                              inv_sum[:, 0:SETH].unsqueeze(2).broadcast_to([P, SETH, P]), ALU.mult
                                              ).then_inc(probs_ready, 1)
                            dve.tensor_tensor(p1[:, :, :], p1[:, :, :],
                                              inv_sum[:, SETH:2 * SETH].unsqueeze(2).broadcast_to([P, SETH, SEQ]), ALU.mult
                                              ).then_inc(probs_ready, 1)
                    return side
                for g in range(4):
                    group(G_MOBA + 4 * s + g, side_of(g), (G_MOBA + 4 * s + g, g % 2))

            moba_set(0, True)
            with dve.Fori(1, MOBA_SETS) as s:
                moba_set(s, False)

            def gain_y(n, parity):
                dve.wait_ge(used, 8 * (G_OUT + n + 1))
                dve.wait_ge(gain_ready, n + 1)
                for t in range(T):
                    dve.wait_ge(y_squared, 2 * n + t + 1)
                    dve.tensor_tensor(y_gain[:, t, n * NC:(n + 1) * NC], ps[:, 2 * parity + t, :],
                                      gain_b[:, n * NC:(n + 1) * NC], ALU.mult).then_inc(y_gained, 1)

            def gain_column(which):
                a = (0, 3 * KT)[which]
                dve.scalar_tensor_tensor(out=gain[:, :], in0=ada_cols[:, a:a + KT], scalar=1.0,
                                         in1=post_cols[:, (2 + which) * KT:(3 + which) * KT], op0=ALU.add, op1=ALU.add
                                         ).then_inc(gain_col, 1)
                dve.wait_ge(gain_col, 2 * which + 1)
                dve.tensor_tensor(gain[:, :], gain[:, :], post_cols[:, which * KT:(which + 1) * KT], ALU.mult
                                  ).then_inc(gain_col, 1)
                dve.wait_ge(gain_col, 2 * which + 2)

            for G in range(G_GA, G_UP):
                phase, n = divmod(G - G_GA, 4)

                def side(h):
                    if h == 6 and G <= G_RETO:
                        keep_chunk(G - 1)
                    if G_RETO < G <= G_MOBAO and h == 3:
                        k = G - 1 - G_RETO
                        dve.wait_ge(used, 8 * G)
                        dve.wait_ge(gate_ready, 2 * MOBA_SETS + 2 * k + 2)
                        for t in range(T):
                            a = gate_a[:, t, k * NC:(k + 1) * NC]
                            dve.tensor_tensor(a, a, ps[:, 2 * ((G - 1) % 2) + t, :], ALU.mult).then_inc(gated, 1)
                    if G_MOBAO < G <= G_OUT and h == 3:
                        k = G - 1 - G_MOBAO
                        dve.wait_ge(used, 8 * G)
                        for t in range(T):
                            b = gate_b[:, t, k * NC:(k + 1) * NC]
                            dve.tensor_tensor(b, b, ps[:, 2 * ((G - 1) % 2) + t, :], ALU.mult).then_inc(gated, 1)
                        dve.wait_ge(gated, 8 + 3 * k + 2)
                        a = gate_a[:, :, k * NC:(k + 1) * NC]
                        dve.tensor_tensor(a, a, gate_b[:, :, k * NC:(k + 1) * NC], ALU.add).then_inc(gated, 1)
                    if n == 3 and phase < 3 and h >= 4:
                        lhs_pair(phase + 1, h - 4, (src_a, src_b, src_a)[phase])
                    if n == 0 and phase > 0:
                        src = (src_a, src_b, src_a)[phase - 1]
                        if (phase < 3 and h < 4) or (phase == 3 and h < 2):
                            lhs_pair(phase, 4 + h, src)
                        if phase == 3 and h >= 6:
                            lhs_pair(phase, h, src)
                    if G == G_MOBAO and h == 4:
                        dve.wait_ge(ada_kept, 4 * D // ADA_BG)
                        gain_column(0)
                    if G_MOBAO <= G < G_OUT and h == 5:
                        k = G - G_MOBAO
                        wait(dve, gain_spread, k - 1)
                        for i in range(4):
                            at = (4 * (k % 2) + i) * P
                            dve.tensor_scalar(diag1[:, at:at + P], ident[:, :], gain[:, 4 * k + i:4 * k + i + 1], None,
                                              ALU.mult).then_inc(gain_diag, 1)
                    if G == G_OUT and h == 4:
                        dve.tensor_tensor(shift2[:, :], ada_cols[:, KT:2 * KT], cols[:, 5 * KT:6 * KT], ALU.add
                                          ).then_inc(mod2, 1)
                        dve.scalar_tensor_tensor(out=scale2[:, :], in0=ada_cols[:, 2 * KT:3 * KT], scalar=1.0,
                                                 in1=cols[:, 6 * KT:7 * KT], op0=ALU.add, op1=ALU.add).then_inc(mod2, 1)
                        dve.wait_ge(mod2, 2)
                        dve.tensor_tensor(scale2[:, :], scale2[:, :], cols[:, 2 * KT:3 * KT], ALU.mult).then_inc(mod2, 1)
                    if G > G_OUT and h == 3:
                        gain_y(G - 1 - G_OUT, (G - 1) % 2)
                group(G, side, (G, G % 2) if G < G_RETO else None)

            def conv(w, out_, c, tile, shift, add):
                src = h_pad[:, c, 2 - shift:2 - shift + SEQ]
                tap = conv_cols[:, 2 - shift, bass.ds(tile, 1)]
                if add is None:
                    return dve.tensor_scalar(out_, src, tap, conv_cols[:, 3, bass.ds(tile, 1)], ALU.mult, ALU.add)
                return dve.scalar_tensor_tensor(out=out_, in0=src, scalar=tap, in1=add, op0=ALU.mult, op1=ALU.add)

            def up_side(j, par_before):
                def side(h):
                    if h == 3:
                        dve.wait_ge(up_low, j)
                        if isinstance(j, int) and j == 1:
                            dve.wait_ge(gain_spread, 5)
                        wait(dve, conv_step, 12 * (j - 1))
                        dve.tensor_tensor(h_pad[:, :, 2:2 + SEQ], ps[:, 4 * par_before:4 * par_before + 4, 0:SEQ],
                                          h_low[:, :, :], ALU.add).then_inc(up_sum, 1)
                    if h in (4, 5, 6):
                        if h == 4:
                            dve.wait_ge(up_sum, j)
                            wait(dve, g_ready, j - 1)
                            if isinstance(j, int) and j == 1:
                                dve.wait_ge(pad_set, 1)
                        for c in range(4):
                            tile = 2 * (j - 1) + c % 2 + (c // 2) * (D_FF // P)
                            acc = h_conv[:, c, :]
                            if h > 4:
                                dve.wait_ge(conv_step, 12 * (j - 1) + 4 * (h - 5) + c + 1)
                            conv(None, acc, c, tile, h - 4, None if h == 4 else acc).then_inc(conv_step, 1)
                    if h == 7:
                        dve.wait_ge(a_ready, j)
                        dve.tensor_tensor(gT[:, bass.ds(2 * (j - 1), 2), :], a_act[:, :, :], h_conv[:, 2:4, :], ALU.mult
                                          ).then_inc(g_ready, 1)
                return side

            def u2_pair(i):
                for kt in (2 * i, 2 * i + 1):
                    dve.wait_ge(x2_turned, i + 1)
                    dve.tensor_scalar(gT[:, kt, :], ps[:, i, (kt % 2) * SEQ:(kt % 2 + 1) * SEQ], scale2[:, kt:kt + 1],
                                      shift2[:, kt:kt + 1], ALU.mult, ALU.add).then_inc(u2_ready, 1)

            def first_up_side(h):
                if h == 3:
                    gain_y(3, 1)
                    dve.wait_ge(y_squared, 8)
                    rstd_of(1, 4)
                    dve.wait_ge(y_gained, 8)
                    dve.wait_ge(x_back, 32)
                    for t in range(T):
                        dve.scalar_tensor_tensor(out=x_sb[:, t, :], in0=y_gain[:, t, :], scalar=rstd[:, t:t + 1],
                                                 in1=x_sb[:, t, :], op0=ALU.mult, op1=ALU.add).then_inc(x2_ready, 1)
                    dve.wait_ge(x2_squared, 2)
                    dve.wait_ge(x2_ready, 2)
                    rstd_of(2, 1)
                    for t in range(T):
                        dve.tensor_scalar(y_gain[:, t, :], x_sb[:, t, :], rstd[:, t:t + 1], None, ALU.mult
                                          ).then_inc(x2_scaled, 1)
                    dve.wait_ge(mod2, 3)
                    for i in range(4):
                        u2_pair(i)
                        lhs_pair(4, i, gT)
                if h > 3:
                    u2_pair(h)
                    lhs_pair(4, h, gT)
                if h == 7:
                    gain_column(1)
                    for i in range(KT):
                        dve.tensor_scalar(diag2[:, i * P:(i + 1) * P], ident[:, :], gain[:, i:i + 1], None, ALU.mult
                                          ).then_inc(gain_diag, 1)

            def second_up_side(h):
                if h == 3:
                    dve.wait_ge(gain_spread, 5)
                    dve.memset(h_pad[:, :, 0:2], 0.0).then_inc(pad_set, 1)
                up_side(1, 0)(h)

            group(G_UP, first_up_side)
            group(G_UP + 1, second_up_side)
            with dve.Fori(1, UPS // 2) as i:
                group(G_UP + 2 * i, up_side(2 * i, 1))
                group(G_UP + 2 * i + 1, up_side(2 * i + 1, 0))

            def g_part(kb, i, parity):
                dve.wait_ge(g_high, 2 * kb + i + 1)
                dve.tensor_tensor(g_lhs[:, parity, 2 * i:2 * i + 2, SEQ:2 * SEQ], gT[:, bass.ds(KB * kb + 2 * i, 2), :],
                                  g_lhs[:, parity, 2 * i:2 * i + 2, 0:SEQ].bitcast(F32), ALU.subtract).then_inc(g_split, 1)

            def down_side(kb, parity, first=False):
                def side(h):
                    if first and h < 2:
                        g_part(0, h, 0)
                    if first:
                        up_side(UPS, 1)(h)
                    if h in (4, 5):
                        g_part(kb + 1, h - 4, 1 - parity)
                return side

            group(G_DOWN, down_side(0, 0, True))
            with dve.Fori(0, (DOWNS - 3) // 2) as i:
                group(G_DOWN + 2 * i + 1, down_side(2 * i + 1, 1))
                group(G_DOWN + 2 * i + 2, down_side(2 * i + 2, 0))
            group(G_DOWN + DOWNS - 2, down_side(DOWNS - 2, 1))
            group(G_DOWN + DOWNS - 1)
            dve.wait_ge(g_ready, UPS)
            for n in range(4):
                dve.wait_ge(used, 8 * (G_DOWN + DOWNS - 1) + 2 * n + 2)
                if n == 0:
                    dve.wait_ge(gain_ready, 5)
                for t in range(T):
                    dve.wait_ge(y2_squared, 2 * n + t + 1)
                    dve.tensor_tensor(y_gain[:, t, n * NC:(n + 1) * NC], ps[:, 2 * n + t, :],
                                      gain_b[:, n * NC:(n + 1) * NC], ALU.mult).then_inc(y2_gained, 1)
            dve.wait_ge(y2_squared, 8)
            rstd_of(3, 4)
            dve.wait_ge(y2_gained, 8)
            for t in range(T):
                for n in range(2):
                    o = y_gain[:, t, n * 1024:(n + 1) * 1024]
                    dve.scalar_tensor_tensor(out=o, in0=o, scalar=rstd[:, t:t + 1], in1=x_sb[:, t, n * 1024:(n + 1) * 1024],
                                             op0=ALU.mult, op1=ALU.add).then_inc(out_ready, 1)


def kernel(**inputs):
    import concourse.bacc as bacc
    from concourse.bass_utils import run_bass_kernel_spmd

    names = ["x", "c", "ada_w", "ada_b", "mix_norm_pre", "mix_norm_post", "w_in", "ret_w_o", "moba_w_o", "w_out",
             "ffn_norm_pre", "ffn_norm_post", "ffn_w_up", "ffn_conv_w", "ffn_conv_b", "ffn_w_down"]
    half = RET_DK // 2
    angle = (np.arange(SEQ, dtype=np.float32)[:, None]
             * (ROPE_BASE ** (-np.arange(half, dtype=np.float32) / half)).astype(np.float32)[None, :])
    by_tile = lambda a: np.ascontiguousarray(a.reshape(T, P, P).transpose(1, 0, 2)).astype(np.float32)
    cos, sin = np.cos(angle), np.sin(angle)
    diff = np.arange(SEQ)[None, :] - np.arange(P)[:, None]
    log_g = np.log1p(-np.exp2(-5.0 - np.arange(RET_HEADS)))
    decay = np.where(diff[:, None, :] >= 0, np.exp(np.maximum(diff, 0)[:, None, :] * log_g[None, :, None]), 0.0)
    tri = np.where(np.arange(P)[None, :] <= np.arange(P)[:, None], 0.0, MASKED)
    tables = {
        "identity": np.eye(P, dtype=np.float32),
        "rope_cos": by_tile(np.concatenate([cos, cos], axis=1)),
        "rope_sin": by_tile(np.concatenate([-sin, sin], axis=1)),
        "causal": np.concatenate([tri, np.zeros((P, P)), tri], axis=1).astype(np.float32),
        "decay": (decay * RET_DK ** -0.5).astype(np.float32),
    }
    nc = bacc.Bacc("TRN2", target_bir_lowering=False, num_devices=1)
    arrays, args = {}, []
    for name in names:
        arrays[f"in_{name}"] = np.ascontiguousarray(inputs[name])
    arrays.update({f"table_{k}": v for k, v in tables.items()})
    for name, a in arrays.items():
        args.append(nc.dram_tensor(name, a.shape, mybir.dt.from_np(a.dtype), kind="ExternalInput").ap())
    args.append(nc.dram_tensor("out", (1, SEQ, D), F32, kind="ExternalOutput").ap())
    hybrid_block(nc, *args)
    result = run_bass_kernel_spmd(nc, [arrays], core_ids=[0])
    return result.results[0]["out"]
```

```python
import math
from contextlib import ExitStack

import numpy as np

import concourse.bass as bass
from concourse import mybir

F32 = mybir.dt.float32
F32R = mybir.dt.float32r
ALU = mybir.AluOpType
ACT = mybir.ActivationFunctionType
AX = mybir.AxisListType

P = 128
SEQ, D = 256, 2048
T = SEQ // P
KT = D // P
RET_HEADS, RET_DK, RET_DV = 8, 128, 256
MOBA_HEADS, MOBA_HD = 16, 128
D_FF = 5632
NORM_EPS, GN_EPS = 1e-6, 1e-5
ROPE_BASE = 10000.0
NC = 512
KB = 4
HB = 8
SETH = 4
COL_RQ, COL_RK, COL_RV, COL_RG, COL_MQ, COL_MK, COL_MV, COL_GA, COL_GB = (
    0, 1024, 2048, 4096, 6144, 8192, 10240, 12288, 14336)
RET_SETS = RET_HEADS // SETH
MOBA_SETS = MOBA_HEADS // SETH
G_FIRST = 3
FIRST_COLS = (COL_RV, COL_RQ, COL_RK)
FIRST_BANKS = (2, 0, 4)
G_MOBA = 6 * RET_SETS
G_GA = G_MOBA + 4 * MOBA_SETS
G_RETO = G_GA + 4
G_MOBAO = G_RETO + 4
G_OUT = G_MOBAO + 4
G_UP = G_OUT + 4
UPS = D_FF // (2 * P)
G_DOWN = G_UP + UPS
DOWNS = D_FF // (KB * P)
ADA_BG = 256
ADA_CHUNKS = 4 * D // ADA_BG
MASKED = -1.7e38


def hybrid_block(nc, x, c, ada_w, ada_b, mix_norm_pre, mix_norm_post, w_in, ret_w_o, moba_w_o, w_out,
                 ffn_norm_pre, ffn_norm_post, ffn_w_up, ffn_conv_w, ffn_conv_b, ffn_w_down,
                 identity, rope_cos, rope_sin, causal, decay_dram, out):
    ctx = ExitStack()

    def sb(name, shape, dt=F32, stack=ctx):
        return stack.enter_context(nc.sbuf_tensor(name, shape, dt))

    def sem(name):
        return ctx.enter_context(nc.semaphore(name))

    def shared(*plans):
        made = {}
        for plan in plans:
            with ExitStack() as part:
                for name, shape, dt in plan:
                    made[name] = sb(name, shape, dt, part)
        return made

    def hold(name, size):
        sb(name, [P, size])

    with ctx:
        stage = sb("stage", [P, 4, KB, NC])
        w_high = sb("w_high", [P, 4, 2, NC], F32R)
        w_low = sb("w_low", [P, 4, 2, NC], F32R)
        lhs = sb("lhs", [P, KT, 2 * SEQ], F32R)
        ident = sb("ident", [P, P])
        ones = sb("ones", [P, P])
        ones_r = sb("ones_r", [P, P], F32R)
        cos2 = sb("cos2", [P, T, P])
        sin2 = sb("sin2", [P, T, P])
        mask = sb("mask", [P, 3 * P])
        cols = sb("cols", [P, 7 * KT])
        c_act = sb("c_act", [P, KT])
        scale1 = sb("scale1", [P, KT])
        shift1 = sb("shift1", [P, KT])
        scale2 = sb("scale2", [P, KT])
        shift2 = sb("shift2", [P, KT])
        gain = sb("gain", [P, KT])
        gain_high = sb("gain_high", [P, KT], F32R)
        gain_low = sb("gain_low", [P, KT], F32R)
        post_cols = sb("post_cols", [P, 4 * KT])
        ada_cols = sb("ada_cols", [P, 4 * KT])
        conv_cols = sb("conv_cols", [P, 4, 88])
        stats = sb("stats", [P, 4, 6])
        moments = sb("moments", [P, 4, 2])
        inv_std = sb("inv_std", [P, 4])
        row_max = sb("row_max", [P, 2 * SETH])
        neg_max = sb("neg_max", [P, 2 * SETH])
        row_sum = sb("row_sum", [P, 2 * SETH])
        inv_sum = sb("inv_sum", [P, 2 * SETH])
        squares = sb("squares", [P, T, 4])
        mean_sq = sb("mean_sq", [P, T])
        rstd = sb("rstd", [P, T])
        spare_root = sb("spare_root", [P, 1])

        m = shared([("x_sb", [P, T, D], F32)],
                   [("gate_b", [P, T, D], F32)])
        x_sb, gate_b = m["x_sb"], m["gate_b"]
        hold("hold_x", T * D)
        rest = ExitStack()
        m = {}

        def region(name, size, *plans):
            m.update(shared(*plans))
            sb(name, [P, size], F32, rest)

        region("hold_m", 4096,
               [("v_ret", [P, T, 1024], F32), ("o_ret", [P, T, 1024], F32)],
               [("src_b", [P, KT, SEQ], F32)],
               [("below_diag1", [P, KT // 2, SEQ], F32), ("diag1", [P, 4 * NC], F32R)])
        region("hold_r", 4096, [("src_a", [P, KT, SEQ], F32)])
        region("hold_q", 8192,
               [("rot", [P, 2, T, NC], F32), ("rot_cos", [P, NC], F32), ("rot_sin", [P, NC], F32),
                ("qT_ret", [P, SETH, SEQ], F32), ("kT_ret", [P, SETH, SEQ], F32),
                ("sT0", [P, SETH, SEQ], F32), ("sT1", [P, SETH, P], F32)],
               [("gate_a", [P, T, D], F32),
                ("qk_nat", [P, T, NC], F32), ("qT", [P, SETH, SEQ], F32),
                ("kT", [P, SETH, SEQ], F32), ("v_moba", [P, T, NC], F32)],
               [("ada_first", [P, 4, KB, NC], F32)])
        region("hold_d", 3072,
               [("decay", [P, RET_HEADS, SEQ], F32), ("gate_r", [P, T, NC], F32)],
               [("p0", [P, SETH, P], F32), ("p1", [P, SETH, SEQ], F32),
                ("pTa", [P, SETH, SEQ], F32), ("pTb", [P, SETH, P], F32)],
               [("rows", [7 * KT, P], F32), ("post_rows", [4 * KT, P], F32), ("conv_rows", [88, 4, P], F32)])
        region("hold_a", 2560,
               [("ada_ring", [P, 2, KB, ADA_BG], F32), ("ada_acc", [P, 2, ADA_BG], F32)],
               [("ada_acc1", [P, 2, 2, NC], F32)])
        rest.close()
        m.update(shared(
            [("gain_b", [P, D], F32), ("y_gain", [P, T, D], F32),
             ("gT", [P, D_FF // P, SEQ], F32), ("g_lhs", [P, 2, KB, 2 * SEQ], F32R)],
            [("below_diag2", [P, (1 + T) * D + 24 * SEQ], F32), ("diag2", [P, 8 * NC], F32R)]))
        with ExitStack() as part:
            sb("skip_gain", [P, D], F32, part)
            for name, shape in (("h_pad", [P, 4, SEQ + 2]), ("h_conv", [P, 4, SEQ]),
                                ("h_low", [P, 4, SEQ]), ("a_act", [P, 2, SEQ])):
                m[name] = sb(name, shape, F32, part)
        v_ret, o_ret, src_b, src_a = m["v_ret"], m["o_ret"], m["src_b"], m["src_a"]
        rot, rot_cos, rot_sin, qT_ret, kT_ret = m["rot"], m["rot_cos"], m["rot_sin"], m["qT_ret"], m["kT_ret"]
        sT0, sT1, gate_a, qk_nat, qT, kT = m["sT0"], m["sT1"], m["gate_a"], m["qk_nat"], m["qT"], m["kT"]
        v_moba, ada_first, decay, gate_r = m["v_moba"], m["ada_first"], m["decay"], m["gate_r"]
        p0, p1, pTa, pTb = m["p0"], m["p1"], m["pTa"], m["pTb"]
        rows, post_rows, conv_rows = m["rows"], m["post_rows"], m["conv_rows"]
        ada_ring, ada_acc, ada_acc1 = m["ada_ring"], m["ada_acc"], m["ada_acc1"]
        gain_b, y_gain, gT, g_lhs = m["gain_b"], m["y_gain"], m["gT"], m["g_lhs"]
        diag1, diag2 = m["diag1"], m["diag2"]
        h_pad, h_conv, h_low, a_act = m["h_pad"], m["h_conv"], m["h_low"], m["a_act"]

        ps = ctx.enter_context(nc.psum_tensor("ps", [P, 8, NC], F32))

        loaded = [sem(f"loaded{b}") for b in range(4)]
        high_ready = sem("high_ready")
        split_ready = sem("split_ready")
        used = sem("used")
        lhs_high = sem("lhs_high")
        lhs_ready = sem("lhs_ready")
        rows_in = sem("rows_in")
        post_rows_in = sem("post_rows_in")
        x_in = [sem("x_in0"), sem("x_in1")]
        consts_in = sem("consts_in")
        ident_in = sem("ident_in")
        decay_in = sem("decay_in")
        ones_set = sem("ones_set")
        cols_turned = sem("cols_turned")
        cols_ready = sem("cols_ready")
        squared = sem("squared")
        norm_sum = sem("norm_sum")
        norm_mean = sem("norm_mean")
        root_loaded = sem("root_loaded")
        norm_root = sem("norm_root")
        norm_inv = sem("norm_inv")
        x_scaled = sem("x_scaled")
        x_turned = sem("x_turned")
        xT_ready = sem("xT_ready")
        ada1_in = [sem(f"ada1_in{b}") for b in range(4)]
        ada1_step = sem("ada1_step")
        ada1_summed = sem("ada1_summed")
        ada1_cols = sem("ada1_cols")
        scale1_ready = sem("scale1_ready")
        u_ready = sem("u_ready")
        ada_in = [sem("ada_in0"), sem("ada_in1")]
        ada_step = sem("ada_step")
        ada_summed = sem("ada_summed")
        ada_kept = sem("ada_kept")
        rot_terms = sem("rot_terms")
        rot_ready = sem("rot_ready")
        rqk_turned = sem("rqk_turned")
        rqk_ready = sem("rqk_ready")
        ret_scored = sem("ret_scored")
        ret_decayed = sem("ret_decayed")
        rv_ready = sem("rv_ready")
        ret_summed = sem("ret_summed")
        gn_stats = sem("gn_stats")
        gn_moments = sem("gn_moments")
        gn_var = sem("gn_var")
        gn_root = sem("gn_root")
        gn_inv = sem("gn_inv")
        gn_ready = sem("gn_ready")
        rg_ready = sem("rg_ready")
        ret_gated = sem("ret_gated")
        ret_turned = sem("ret_turned")
        ret_kept = sem("ret_kept")
        mqk_nat = sem("mqk_nat")
        mqk_turned = sem("mqk_turned")
        mqk_ready = sem("mqk_ready")
        scored = sem("scored")
        masked = sem("masked")
        maxed = sem("maxed")
        neg_ready = sem("neg_ready")
        exp_ready = sem("exp_ready")
        inv_ready = sem("inv_ready")
        probs_ready = sem("probs_ready")
        probs_turned = sem("probs_turned")
        probsT_ready = sem("probsT_ready")
        mv_ready = sem("mv_ready")
        attended = sem("attended")
        att_kept = sem("att_kept")
        gate_ready = sem("gate_ready")
        gated = sem("gated")
        merge_turned = sem("merge_turned")
        merge_kept = sem("merge_kept")
        gain_col = sem("gain_col")
        gain_diag = sem("gain_diag")
        gain_spread = sem("gain_spread")
        gain_ready = sem("gain_ready")
        x_back = sem("x_back")
        y_squared = sem("y_squared")
        y_gained = sem("y_gained")
        x2_ready = sem("x2_ready")
        x2_squared = sem("x2_squared")
        rstd_diag = sem("rstd_diag")
        x2_turned = sem("x2_turned")
        x2_normed = sem("x2_normed")
        row_spread = sem("row_spread")
        row_ready = sem("row_ready")
        u2_ready = sem("u2_ready")
        mod2 = sem("mod2")
        pad_set = sem("pad_set")
        up_low = sem("up_low")
        up_sum = sem("up_sum")
        conv_step = sem("conv_step")
        a_ready = sem("a_ready")
        g_ready = sem("g_ready")
        g_high = sem("g_high")
        g_split = sem("g_split")
        y2_squared = sem("y2_squared")
        y2_gained = sem("y2_gained")
        out_ready = sem("out_ready")
        stored = sem("stored")

        block = ctx.enter_context(nc.Block())

        diag_rstd, rstd_row = gT[:, 42, :], gT[:, 43, :]

        vectors = (c[0], mix_norm_pre[0], ffn_norm_pre[0], ada_b[0, 0:D], ada_b[0, D:2 * D], ada_b[0, 3 * D:4 * D],
                   ada_b[0, 4 * D:5 * D])

        def wait(engine, semaphore, value):
            if not isinstance(value, int) or value > 0:
                engine.wait_ge(semaphore, value)

        def moba_out_of_psum(s, g):
            return ((mqk_nat, 4 * s + 2), (mqk_nat, 4 * s + 4), (mv_ready, 2 * s + 2), (gate_ready, 2 * s + 2))[g]

        def out_of_psum(G):
            if G < 0:
                return None
            if G < G_MOBA:
                s, g = divmod(G, 6)
                if G == 1:
                    return rv_ready, 2
                if G == 2:
                    return rot_ready, 2
                return ((rot_ready, 4 * s + 2), (rot_ready, 4 * s + 4), (rv_ready, 4 * s + 2),
                        (rv_ready, 4 * s + 4), (rg_ready, 2 * s + 1), (rg_ready, 2 * s + 2))[g]
            if G < G_GA:
                return moba_out_of_psum(*divmod(G - G_MOBA, 4))
            phase, n = divmod(G - G_GA, 4)
            return ((gate_ready, 2 * MOBA_SETS + 2 * n + 2), (gated, 2 * n + 2), (gated, 8 + 3 * n + 2),
                    (y_gained, 2 * n + 2))[phase]

        def w_tile(w, kb, col):
            return w[0, kb * KB * P:(kb + 1) * KB * P, bass.ds(col, NC)].rearrange("(k p) n -> p k n", p=P)

        @block.sync
        def _(sp):
            for n in range(4):
                sp.dma_start(rows[n * KT:(n + 1) * KT, :], vectors[n].rearrange("(k p) -> k p", p=P)).then_inc(rows_in, 16)

            def first_chunk(kb, which, n):
                for b in range(4):
                    wait(sp, ada1_step, KT * (n - 1) + KB * (b + 1))
                    sp.dma_start(ada_first[:, b, :, :], w_tile(ada_w, b, kb * NC + which * D)).then_inc(ada1_in[b], 16)

            for kb in range(KT // KB):
                first_chunk(kb, 0, 2 * kb)
                if kb == 0:
                    for t in range(T):
                        sp.dma_start(x_sb[:, t, :], x[0, t * P:(t + 1) * P, :]).then_inc(x_in[t], 16)
                for g, col in enumerate(FIRST_COLS):
                    if g == 1:
                        first_chunk(kb, 1, 2 * kb + 1)
                    m_ = G_FIRST * kb + g
                    wait(sp, split_ready, 2 * (m_ - 4) + 2)
                    sp.dma_start(stage[:, m_ % 4, :, :], w_tile(w_in, kb, col)).then_inc(loaded[m_ % 4], 16)

            def load(w, G, col):
                for b in range(4):
                    sp.wait_ge(split_ready, 8 * G - 8 + 2 * b + 2)
                    sp.dma_start(stage[:, b, :, :], w_tile(w, b, col)).then_inc(loaded[b], 16)

            for s in range(RET_SETS):
                for g, col in enumerate((COL_RQ + s * NC, COL_RK + s * NC, COL_RV + s * 2 * NC,
                                         COL_RV + s * 2 * NC + NC, COL_RG + s * 2 * NC, COL_RG + s * 2 * NC + NC)):
                    if 6 * s + g >= G_FIRST:
                        load(w_in, 6 * s + g, col)
            with sp.Fori(0, MOBA_SETS) as s:
                for g, col in enumerate((COL_MQ, COL_MK, COL_MV, COL_GB)):
                    load(w_in, G_MOBA + 4 * s + g, col + s * NC)
            for w, G0, col in ((w_in, G_GA, COL_GA), (ret_w_o, G_RETO, 0), (moba_w_o, G_MOBAO, 0), (w_out, G_OUT, 0)):
                with sp.Fori(0, 4) as n:
                    load(w, G0 + n, col + n * NC)
            up = ffn_w_up[0].rearrange("(k p) (c n) -> p k c n", p=P, c=2)
            with sp.Fori(0, UPS) as j:
                for b in range(4):
                    sp.wait_ge(split_ready, 8 * (G_UP + j) - 8 + 2 * b + 2)
                    for half in range(2):
                        sp.dma_start(stage[:, b, :, half * 2 * P:(half + 1) * 2 * P],
                                     up[:, b * KB:(b + 1) * KB, half, bass.ds(j * 2 * P, 2 * P)]).then_inc(loaded[b], 16)
            down = ffn_w_down[0].rearrange("(k p) n -> p k n", p=P)
            with sp.Fori(0, DOWNS) as kb:
                for n in range(4):
                    sp.wait_ge(split_ready, 8 * (G_DOWN + kb) - 8 + 2 * n + 2)
                    sp.dma_start(stage[:, n, :, :],
                                 down[:, bass.ds(kb * KB, KB), n * NC:(n + 1) * NC]).then_inc(loaded[n], 16)
            for t in range(T):
                for n in range(4):
                    sp.wait_ge(out_ready, 4 * t + n + 1)
                    sp.dma_start(out[0, t * P:(t + 1) * P, n * NC:(n + 1) * NC],
                                 y_gain[:, t, n * NC:(n + 1) * NC]).then_inc(stored, 16)
            sp.wait_ge(stored, 16 * 4 * T)

        @block.gpsimd
        def _(pool):
            pool.memset(ones[:, :], 1.0).then_inc(ones_set, 1)
            for n, src in enumerate((mix_norm_post[0], ffn_norm_post[0], ada_b[0, 2 * D:3 * D], ada_b[0, 5 * D:6 * D])):
                pool.dma_start(post_rows[n * KT:(n + 1) * KT, :],
                              src.rearrange("(k p) -> k p", p=P)).then_inc(post_rows_in, 16)
            for n in range(3):
                pool.dma_start(conv_rows[:, n, :], ffn_conv_w[0, n].rearrange("(k p) -> k p", p=P)).then_inc(post_rows_in, 16)
            pool.dma_start(conv_rows[:, 3, :], ffn_conv_b[0].rearrange("(k p) -> k p", p=P)).then_inc(post_rows_in, 16)
            bg = ada_w[0].rearrange("(k p) n -> p k n", p=P)

            def chunk(j):
                for q in range(4):
                    if isinstance(j, int) and 4 * j + q == 0:
                        pool.wait_ge(ada1_cols, 8)
                    elif not isinstance(j, int) or 4 * j + q > 1:
                        pool.wait_ge(ada_step, 16 * j + 4 * q - 4)
                    pool.dma_start(ada_ring[:, q % 2, :, :],
                                   bg[:, q * KB:(q + 1) * KB, bass.ds(j * ADA_BG + 2 * D, ADA_BG)]
                                   ).then_inc(ada_in[q % 2], 16)
            chunk(0)
            with pool.Fori(1, ADA_CHUNKS) as j:
                chunk(j)

        @block.tensor
        def _(pe):
            def multiply(kt, bank, slot, k):
                for t in range(T):
                    acc = ps[:, bank + t, :]
                    hi = lhs[:, kt, t * P:(t + 1) * P]
                    lo = lhs[:, kt, SEQ + t * P:SEQ + (t + 1) * P]
                    pe.matmul(acc, hi, w_high[:, slot, k, :], start=kt == 0, stop=False)
                    pe.matmul(acc, hi, w_low[:, slot, k, :], start=False, stop=False)
                    last = pe.matmul(acc, lo, w_high[:, slot, k, :], start=False, stop=kt == KT - 1)
                return last

            def product(G, parity, out_before=None, lhs_phase=None, side=None):
                for h in range(HB):
                    if h == 0 and out_before is not None:
                        pe.wait_ge(*out_before)
                    if lhs_phase is not None:
                        pe.wait_ge(lhs_ready, 8 * lhs_phase + h + 1)
                    pe.wait_ge(split_ready, 8 * G + h + 1)
                    for k in range(2):
                        last = multiply(2 * h + k, 2 * parity, h % 4, k)
                    last.then_inc(used, 1)
                    if side is not None:
                        side(h)

            def turn(bank, tiles):
                for n, tile in enumerate(tiles):
                    last = pe.transpose(ps[:, bank, n * P:(n + 1) * P], tile, ident[:, :])
                return last

            def sum_chunk(j, parity):
                pe.wait_ge(ada_step, 16 * j + 16)
                if not (isinstance(j, int) and j == 0):
                    pe.wait_ge(ada_kept, j)
                for n in range(2):
                    last = pe.matmul(ps[:, 7, n:n + 1], ada_acc[:, parity, n * P:(n + 1) * P], ones[:, 0:1],
                                     start=True, stop=True)
                last.then_inc(ada_summed, 1)

            pe.wait_ge(ident_in, 16)
            pe.wait_ge(rows_in, 16 * 7)
            pe.transpose(ps[:, 4, 0:7 * KT], rows[:, :], ident[0:7 * KT, 0:7 * KT]).then_inc(cols_turned, 1)
            def turn_x():
                pe.wait_ge(x_scaled, 2)
                for pair in range(KT // 2):
                    wait(pe, xT_ready, pair - 3)
                    turn(pair % 4, [x_sb[:, t, (2 * pair + k) * P:(2 * pair + k + 1) * P]
                                    for k in range(2) for t in range(T)]).then_inc(x_turned, 1)

            pe.wait_ge(ones_set, 1)

            def sum_first(n, which):
                wait(pe, ada1_cols, n - 1)
                pe.wait_ge(ada1_step, KT * (n + 1))
                for i in range(4):
                    for e in range(2):
                        last = pe.matmul(ps[:, 6 + which, i:i + 1], ada_acc1[:, which, e, i * P:(i + 1) * P], ones[:, 0:1],
                                         start=e == 0, stop=e == 1)
                last.then_inc(ada1_summed, 1)

            def grow_first(kb):
                for g in range(G_FIRST):
                    for half in range(2):
                        n = 2 * (G_FIRST * kb + g) + half
                        pe.wait_ge(lhs_ready, 2 * kb + half + 1)
                        pe.wait_ge(split_ready, n + 1)
                        if n == 4:
                            pe.wait_ge(cols_ready, 4)
                        for k in range(2):
                            kt = KB * kb + 2 * half + k
                            last = multiply(kt, FIRST_BANKS[g], n % 4, k)
                        last.then_inc(used, 1)
                        if (g, half) == (2, 0) and kb + 1 < KT // KB:
                            sum_first(2 * kb + 2, 0)

            sum_first(0, 0)
            turn_x()
            pe.wait_ge(post_rows_in, 16 * 8)
            pe.transpose(ps[:, 5, 352:352 + 4 * KT], post_rows[:, :], ident[0:4 * KT, 0:4 * KT])
            for n in range(4):
                last = pe.transpose(ps[:, 5, n * 88:(n + 1) * 88], conv_rows[:, n, :], ident[0:88, 0:88])
            last.then_inc(cols_turned, 1)
            for kb in range(KT // KB):
                sum_first(2 * kb + 1, 1)
                grow_first(kb)
            def ret_side(G):
                def side(h):
                    if h == 1 and G > G_FIRST:
                        sum_chunk(G - 1 - G_FIRST, G % 2)
                    for s in range(RET_SETS):
                        g = G - 6 * s
                        if (g, h) in ((3, 3), (3, 6)):
                            n = 2 * s + h // 6
                            pe.wait_ge(rot_ready, 2 * n + 2)
                            if n == 0:
                                pe.wait_ge(rot_ready, 4)
                            elif n % 2 == 0:
                                pe.wait_ge(ret_kept, 2 * s)
                            else:
                                pe.wait_ge(rqk_ready, n)
                            for b in range(2):
                                last = turn(4 + b, [rot[:, n % 2, t, (2 * b + hd) * P:(2 * b + hd + 1) * P]
                                                    for hd in range(2) for t in range(T)])
                            last.then_inc(rqk_turned, 1)
                        if (g, h) == (4, 1):
                            pe.wait_ge(rqk_ready, 2 * s + 2)
                            for hd in range(SETH):
                                pe.matmul(ps[:, 5 + hd // 2, hd % 2 * SEQ:(hd % 2 + 1) * SEQ], kT_ret[:, hd, 0:P],
                                          qT_ret[:, hd, :], start=True, stop=True)
                                last = pe.matmul(ps[:, 4, hd * P:(hd + 1) * P], kT_ret[:, hd, P:SEQ],
                                                 qT_ret[:, hd, P:SEQ], start=True, stop=True)
                            last.then_inc(ret_scored, 1)
                        if (g, h) in ((4, 4), (5, 1)):
                            n = 2 * s + g - 4
                            if g == 4:
                                pe.wait_ge(ret_decayed, 2 * s + 2)
                            else:
                                pe.wait_ge(gn_ready, 4 * n)
                            pe.wait_ge(rv_ready, 2 * n + 2)
                            for i in range(2):
                                hd = 2 * (g - 4) + i
                                v0, v1 = (v_ret[:, t, hd * RET_DV:(hd + 1) * RET_DV] for t in range(T))
                                pe.matmul(ps[:, 4 + i, 0:RET_DV], sT0[:, hd, 0:P], v0, start=True, stop=True)
                                pe.matmul(ps[:, 4 + i, RET_DV:2 * RET_DV], sT0[:, hd, P:SEQ], v0, start=True, stop=False)
                                last = pe.matmul(ps[:, 4 + i, RET_DV:2 * RET_DV], sT1[:, hd, :], v1,
                                                 start=False, stop=True)
                            last.then_inc(ret_summed, 1)
                        if (g, h) in ((5, 6), (6, 2)):
                            n = 2 * s + g - 5
                            pe.wait_ge(ret_gated, n + 1)
                            if g == 5:
                                pe.wait_ge(gn_ready, 8 * s + 8)
                            else:
                                pe.wait_ge(ret_kept, n)
                            for b in range(2):
                                at = (g - 5) * NC + 2 * b * P
                                last = turn(4 + b, [o_ret[:, t, at + e * P:at + (e + 1) * P]
                                                    for e in range(2) for t in range(T)])
                            last.then_inc(ret_turned, 1)
                return side

            for G in range(G_FIRST, G_MOBA):
                product(G, G % 2, out_of_psum(G - 2), None, ret_side(G))

            def moba_set(s, first):
                def side_of(g):
                    ret = ret_side(G_MOBA) if first and g == 0 else None

                    def side(h):
                        if ret is not None:
                            ret(h)
                        elif h == 1:
                            sum_chunk(G_MOBA + 4 * s + g - 1 - G_FIRST, g % 2)
                        if (g, h) in ((1, 1), (2, 1)):
                            if g == 1 and not first:
                                pe.wait_ge(att_kept, s)
                            if g == 1 and first:
                                pe.wait_ge(ret_kept, 2 * RET_SETS)
                            if g == 2:
                                pe.wait_ge(mqk_ready, 2 * s + 1)
                            pe.wait_ge(mqk_nat, 4 * s + 2 * g)
                            for b in range(2):
                                last = turn(4 + b, [qk_nat[:, t, (2 * b + hd) * P:(2 * b + hd + 1) * P]
                                                    for hd in range(2) for t in range(T)])
                            last.then_inc(mqk_turned, 1)
                        if (g, h) == (2, 4):
                            pe.wait_ge(mqk_ready, 2 * s + 2)
                            for hd in range(SETH):
                                pe.matmul(ps[:, 4, hd * P:(hd + 1) * P], qT[:, hd, 0:P], kT[:, hd, 0:P],
                                          start=True, stop=True)
                                last = pe.matmul(ps[:, 5 + hd // 2, hd % 2 * SEQ:(hd % 2 + 1) * SEQ], qT[:, hd, P:SEQ],
                                                 kT[:, hd, :], start=True, stop=True)
                            last.then_inc(scored, 1)
                        if (g, h) == (3, 4):
                            pe.wait_ge(probs_ready, 2 * s + 2)
                            turn(4, [p0[:, hd, :] for hd in range(SETH)])
                            for b in range(2):
                                last = turn(5 + b, [p1[:, 2 * b + hd, kk * P:(kk + 1) * P]
                                                    for hd in range(2) for kk in range(2)])
                            last.then_inc(probs_turned, 1)
                        if (g, h) == (3, 7):
                            pe.wait_ge(probsT_ready, 3 * s + 3)
                            pe.wait_ge(mv_ready, 2 * s + 2)
                            for hd in range(SETH):
                                o = ps[:, 4 + hd // 2, hd % 2 * SEQ:(hd % 2 + 1) * SEQ]
                                pe.matmul(o, v_moba[:, 0, hd * P:(hd + 1) * P], pTa[:, hd, :], start=True, stop=False)
                                last = pe.matmul(o[:, P:SEQ], v_moba[:, 1, hd * P:(hd + 1) * P], pTb[:, hd, :],
                                                 start=False, stop=True)
                            last.then_inc(attended, 1)
                    return side
                for g in range(4):
                    if g >= 2:
                        before = moba_out_of_psum(s, g - 2)
                    else:
                        before = out_of_psum(G_MOBA + g - 2) if first else moba_out_of_psum(s - 1, g + 2)
                    product(G_MOBA + 4 * s + g, g % 2, before, None, side_of(g))

            moba_set(0, True)
            with pe.Fori(1, MOBA_SETS) as s:
                moba_set(s, False)

            def spread(bank, diag, n):
                pe.matmul(ps[:, bank, :], ones_r[:, :], diag[:, 2 * n * NC:(2 * n + 1) * NC], start=True, stop=False)
                return pe.matmul(ps[:, bank, :], ones_r[:, :], diag[:, (2 * n + 1) * NC:(2 * n + 2) * NC],
                                 start=False, stop=True)

            def spread_gain(n):
                pe.wait_ge(gain_diag, 8 * n + 8)
                if n:
                    pe.wait_ge(gain_ready, n)
                last = spread(6, diag1, n % 2)
                last.then_inc(gain_spread, 1)

            for G in range(G_GA, G_UP):
                def side(h):
                    if h == 1 and G <= G_FIRST + ADA_CHUNKS:
                        sum_chunk(G - 1 - G_FIRST, G % 2)
                    if G > G_MOBAO and G <= G_OUT and h == 1:
                        n = G - 1 - G_MOBAO
                        pe.wait_ge(gated, 8 + 3 * (n + 1))
                        if n == 0:
                            pe.wait_ge(att_kept, MOBA_SETS)
                        else:
                            pe.wait_ge(merge_kept, n)
                        for b in range(2):
                            last = turn(4 + b, [gate_a[:, t, (4 * n + 2 * b + e) * P:(4 * n + 2 * b + e + 1) * P]
                                                for e in range(2) for t in range(T)])
                        last.then_inc(merge_turned, 1)
                    if G_MOBAO <= G < G_OUT and h == 4:
                        spread_gain(G - G_MOBAO)
                phase = (G - G_RETO) // 4 + 1 if G >= G_RETO and (G - G_RETO) % 4 == 0 else None
                product(G, G % 2, out_of_psum(G - 2), phase, side)

            def turn_x2(pair):
                pe.wait_ge(x2_ready, 2 * (pair // 4) + 2)
                if pair == 3:
                    pe.wait_ge(row_ready, 1)
                if pair > 3:
                    pe.wait_ge(x2_normed, pair - 3)
                turn(4 + pair % 4, [x_sb[:, t, (2 * pair + k) * P:(2 * pair + k + 1) * P] for k in range(2) for t in range(T)]
                     ).then_inc(x2_turned, 1)

            pe.wait_ge(merge_kept, 4)
            pe.wait_ge(gain_ready, 4)
            for pair in range(3):
                turn_x2(pair)
            pe.wait_ge(rstd_diag, 2)
            pe.matmul(ps[:, 7, 0:SEQ], ones[:, :], diag_rstd, start=True, stop=True).then_inc(row_spread, 1)
            turn_x2(3)

            def up_product(j, parity, first):
                G = G_UP + j
                for h in range(HB):
                    if h == 0:
                        if first and parity == 0:
                            pe.wait_ge(y_gained, 8)
                        elif first:
                            pe.wait_ge(gain_ready, 5)
                        else:
                            pe.wait_ge(up_sum, j - 1)
                    if first and parity == 0:
                        pe.wait_ge(lhs_ready, 8 * 4 + h + 1)
                    pe.wait_ge(split_ready, 8 * G + h + 1)
                    for k in range(2):
                        kt = 2 * h + k
                        for ct in range(4):
                            pe.matmul(ps[:, 4 * parity + ct, :], w_high[:, h % 4, k, ct * P:(ct + 1) * P], lhs[:, kt, :],
                                      start=kt == 0, stop=False)
                            last = pe.matmul(ps[:, 4 * parity + ct, 0:SEQ], w_low[:, h % 4, k, ct * P:(ct + 1) * P],
                                             lhs[:, kt, 0:SEQ], start=False, stop=kt == KT - 1)
                    last.then_inc(used, 1)
                    if first and parity == 0 and h < 4:
                        turn_x2(4 + h)
                    if first and parity == 0 and h == 6:
                        pe.wait_ge(x2_normed, KT // 2)
                        pe.wait_ge(gain_diag, 4 * KT)
                        for n in range(4):
                            last = spread(4 + n, diag2, n)
                        last.then_inc(gain_spread, 1)

            up_product(0, 0, True)
            up_product(1, 1, True)
            with pe.Fori(1, UPS // 2) as i:
                up_product(2 * i, 0, False)
                up_product(2 * i + 1, 1, False)

            def down_step(kb, parity, first=False, final=False):
                G = G_DOWN + kb
                for h in range(HB):
                    n = h // 2
                    if h < 2:
                        pe.wait_ge(g_split, 2 * kb + h + 1)
                    if first and h == 0:
                        pe.wait_ge(up_sum, UPS - 1)
                    if first and h == 4:
                        pe.wait_ge(up_sum, UPS)
                    pe.wait_ge(split_ready, 8 * G + h + 1)
                    for k in range(2):
                        kk = 2 * (h % 2) + k
                        for t in range(T):
                            acc = ps[:, 2 * n + t, :]
                            hi = g_lhs[:, parity, kk, t * P:(t + 1) * P]
                            lo = g_lhs[:, parity, kk, SEQ + t * P:SEQ + (t + 1) * P]
                            pe.matmul(acc, hi, w_high[:, h % 4, k, :], start=first and kk == 0, stop=False)
                            pe.matmul(acc, hi, w_low[:, h % 4, k, :], start=False, stop=False)
                            last = pe.matmul(acc, lo, w_high[:, h % 4, k, :], start=False, stop=final and kk == 3)
                    last.then_inc(used, 1)

            down_step(0, 0, first=True)
            with pe.Fori(0, (DOWNS - 3) // 2) as i:
                down_step(2 * i + 1, 1)
                down_step(2 * i + 2, 0)
            down_step(DOWNS - 2, 1)
            down_step(DOWNS - 1, 0, final=True)

        @block.scalar
        def _(act):
            def high_part(n, slot, h, load_count):
                if h % 2 == 0:
                    act.wait_ge(loaded[slot], load_count)
                wait(act, used, n - 3)
                act.activation(w_high[:, h % 4, :, :], stage[:, slot, 2 * (h % 2):2 * (h % 2) + 2, :],
                               ACT.Copy).then_inc(high_ready, 1)

            def group(G, side=None, loads=None):
                for h in range(HB):
                    high_part(8 * G + h, h // 2, h, 16 * (G + 1 if loads is None else loads))
                    if side is not None:
                        side(h)

            def lhs_pair(phase, i, src, G_before):
                wait(act, used, 8 * G_before + i + 1)
                act.activation(lhs[:, 2 * i:2 * i + 2, 0:SEQ], src[:, 2 * i:2 * i + 2, :], ACT.Copy
                               ).then_inc(lhs_high, 1)

            def load_root_table():
                act.wait_ge(ones_set, 1)
                act.activation(spare_root[:, :], ones[:, 0:1], ACT.Sqrt).then_inc(root_loaded, 1)

            def root_of_norm(k):
                act.wait_ge(norm_mean, k + 1)
                act.activation(rstd[:, :], rstd[:, :], ACT.Sqrt).then_inc(norm_root, 1)

            act.dma_start(ident[:, :], identity[:, :]).then_inc(ident_in, 16)
            for n in range(4, 7):
                act.dma_start(rows[n * KT:(n + 1) * KT, :], vectors[n].rearrange("(k p) -> k p", p=P)).then_inc(rows_in, 16)
            act.wait_ge(cols_turned, 1)
            act.activation(c_act[:, :], ps[:, 4, 0:KT], ACT.Silu).then_inc(cols_ready, 1)
            act.activation(cols[:, :], ps[:, 4, 0:7 * KT], ACT.Copy).then_inc(cols_ready, 1)
            junk = src_b[:, 0:8, :].rearrange("p k n -> p (k n)")
            for t in range(T):
                act.wait_ge(x_in[t], 16)
                if t:
                    act.wait_ge(squared, t)
                act.activation(junk, x_sb[:, t, :], ACT.Square, accum_out=squares[:, t, 0:1]).then_inc(squared, 1)
            root_of_norm(0)
            act.wait_ge(norm_inv, 1)
            for t in range(T):
                act.activation(x_sb[:, t, :], x_sb[:, t, :], ACT.Copy, scale=rstd[:, t:t + 1]).then_inc(x_scaled, 1)
            for i in range(KT // 2):
                act.wait_ge(x_turned, i + 1)
                act.activation(src_a[:, 2 * i:2 * i + 2, :], ps[:, i % 4, :].rearrange("p (k n) -> p k n", k=2),
                               ACT.Copy).then_inc(xT_ready, 1)
            act.wait_ge(cols_turned, 2)
            act.activation(post_cols[:, :], ps[:, 5, 352:352 + 4 * KT], ACT.Copy).then_inc(cols_ready, 1)
            act.activation(conv_cols[:, :, :], ps[:, 5, 0:352].rearrange("p (n k) -> p n k", n=4), ACT.Copy
                           ).then_inc(cols_ready, 1)

            def keep_v(n, done, bank):
                act.wait_ge(used, done)
                wait(act, ret_summed, n // 2 * 2)
                for t in range(T):
                    act.activation(v_ret[:, t, n % 2 * NC:(n % 2 + 1) * NC], ps[:, bank + t, :], ACT.Copy
                                   ).then_inc(rv_ready, 1)

            for kb in range(KT // KB):
                for n in range(2 * G_FIRST * kb, 2 * G_FIRST * (kb + 1)):
                    if n == 2 * G_FIRST * kb + 2:
                        for i in range(2):
                            act.wait_ge(u_ready, KB * kb + 2 * i + 2)
                            lhs_pair(0, 2 * kb + i, src_b, -1)
                    high_part(n, n // 2 % 4, n, 16 * (n // 8 + 1))
            act.dma_start(cos2[:, :, :], rope_cos[:, :, :]).then_inc(consts_in, 16)
            act.dma_start(sin2[:, :, :], rope_sin[:, :, :]).then_inc(consts_in, 16)
            act.dma_start(mask[:, :], causal[:, :]).then_inc(consts_in, 16)
            act.dma_start(decay[:, :, :], decay_dram[:, :, :]).then_inc(decay_in, 16)
            keep_v(0, 8 * G_FIRST - 4, FIRST_BANKS[0])

            def ret_side(G):
                def side(h):
                    for s in range(RET_SETS):
                        g = G - 6 * s
                        if (g, h) in ((3, 7), (4, 2)):
                            n = 2 * s + g - 3
                            act.wait_ge(rqk_turned, n + 1)
                            wait(act, ret_scored, s)
                            act.activation((qT_ret, kT_ret)[g - 3][:, :, :],
                                           ps[:, 4:6, :].rearrange("p b (h n) -> p (b h) n", h=2),
                                           ACT.Copy).then_inc(rqk_ready, 1)
                        if h == 3 and g in (3, 4) and G > G_FIRST:
                            keep_v(2 * s + g - 3, 8 * G, 2 * ((G - 1) % 2))
                        if (g, h) in ((5, 0), (5, 5)):
                            n = 2 * s + h // 5
                            act.wait_ge(gn_var, n + 1)
                            act.activation(inv_std[:, :], inv_std[:, :], ACT.Sqrt).then_inc(gn_root, 1)
                        if h == 3 and g in (5, 6):
                            n = 2 * s + g - 5
                            act.wait_ge(used, 8 * G)
                            wait(act, ret_gated, n)
                            act.activation(gate_r[:, :, :], ps[:, 2 * ((G - 1) % 2):2 * ((G - 1) % 2) + 2, :],
                                           ACT.Silu).then_inc(rg_ready, 1)
                        if (g, h) in ((6, 2), (6, 6)):
                            n = 2 * s + h // 6
                            act.wait_ge(ret_turned, n + 1)
                            act.activation(src_a[:, 4 * n:4 * n + 4, :],
                                           ps[:, 4:6, :].rearrange("p b (k n) -> p (b k) n", k=2),
                                           ACT.Copy).then_inc(ret_kept, 1)
                return side

            for G in range(G_FIRST, G_MOBA):
                group(G, ret_side(G))

            def keep_attended(s):
                act.wait_ge(attended, s + 1)
                act.activation(src_b[:, bass.ds(SETH * s, SETH), :], ps[:, 4:6, :].rearrange("p b (h n) -> p (b h) n", h=2),
                               ACT.Copy).then_inc(att_kept, 1)

            def keep_gate(gate, G_next, parity, col):
                act.wait_ge(used, 8 * G_next)
                for t in range(T):
                    act.activation(gate[:, t, bass.ds(col, NC)], ps[:, 2 * parity + t, :], ACT.Sigmoid
                                   ).then_inc(gate_ready, 1)

            def moba_set(s, first):
                def side_of(g):
                    ret = ret_side(G_MOBA) if first and g == 0 else None
                    G = G_MOBA + 4 * s + g

                    def side(h):
                        if ret is not None:
                            ret(h)
                        if (g, h) == (0, 3) and not first:
                            keep_attended(s - 1)
                            keep_gate(gate_b, G, 1, (s - 1) * NC)
                        if h == 3 and g in (1, 2):
                            act.wait_ge(used, 8 * G)
                            if not (first and g == 1):
                                act.wait_ge(mqk_turned, 2 * s + g - 1)
                            for t in range(T):
                                act.activation(qk_nat[:, t, :], ps[:, 2 * (1 - g % 2) + t, :], ACT.Copy
                                               ).then_inc(mqk_nat, 1)
                        if h == 5 and g in (1, 2):
                            act.wait_ge(mqk_turned, 2 * s + g)
                            if not first:
                                act.wait_ge(scored, s)
                            act.activation((qT, kT)[g - 1][:, :, :], ps[:, 4:6, :].rearrange("p b (h n) -> p (b h) n", h=2),
                                           ACT.Copy).then_inc(mqk_ready, 1)
                        if (g, h) == (3, 2):
                            act.wait_ge(neg_ready, s + 1)
                            for hd in range(SETH):
                                act.activation(p0[:, hd, :], p0[:, hd, :], ACT.Exp, bias=neg_max[:, hd:hd + 1],
                                               accum_out=row_sum[:, hd:hd + 1]).then_inc(exp_ready, 1)
                            for hd in range(SETH):
                                n = SETH + hd
                                act.activation(p1[:, hd, :], p1[:, hd, :], ACT.Exp, bias=neg_max[:, n:n + 1],
                                               accum_out=row_sum[:, n:n + 1]).then_inc(exp_ready, 1)
                        if (g, h) == (3, 3):
                            act.wait_ge(used, 8 * G)
                            if not first:
                                act.wait_ge(attended, s)
                            for t in range(T):
                                act.activation(v_moba[:, t, :], ps[:, t, :], ACT.Copy).then_inc(mv_ready, 1)
                        if (g, h) == (3, 6):
                            act.wait_ge(probs_turned, s + 1)
                            if not first:
                                act.wait_ge(attended, s)
                            act.activation(pTa[:, :, 0:P], ps[:, 4, :].rearrange("p (h n) -> p h n", h=SETH),
                                           ACT.Copy).then_inc(probsT_ready, 1)
                            act.activation(pTa[:, :, P:SEQ], ps[:, 5:7, :].rearrange("p b (h n) -> p (b h) n", h=2)[:, :, 0:P],
                                           ACT.Copy).then_inc(probsT_ready, 1)
                            act.activation(pTb[:, :, :], ps[:, 5:7, :].rearrange("p b (h n) -> p (b h) n", h=2)[:, :, P:SEQ],
                                           ACT.Copy).then_inc(probsT_ready, 1)
                    return side
                for g in range(4):
                    group(G_MOBA + 4 * s + g, side_of(g))

            moba_set(0, True)
            with act.Fori(1, MOBA_SETS) as s:
                moba_set(s, False)

            def square_y(n, parity):
                act.wait_ge(used, 8 * (G_OUT + n + 1))
                for t in range(T):
                    wait(act, y_squared, 2 * n + t)
                    if n == 3 and t == 1:
                        act.wait_ge(y_gained, 7)
                    act.activation(gT[:, 40:42, :].rearrange("p k n -> p (k n)"), ps[:, 2 * parity + t, :], ACT.Square,
                                   accum_out=squares[:, t, n:n + 1]).then_inc(y_squared, 1)

            def source_kept(phase, i):
                return ((ret_kept, 2 * RET_SETS), (att_kept, MOBA_SETS), (merge_kept, i // 2 + 1))[phase - 1]

            for G in range(G_GA, G_UP):
                phase, n = divmod(G - G_GA, 4)

                def side(h):
                    if G == G_GA and h == 3:
                        keep_attended(MOBA_SETS - 1)
                        keep_gate(gate_b, G, 1, (MOBA_SETS - 1) * NC)
                    if G_GA < G <= G_RETO and h == 3:
                        keep_gate(gate_a, G, (G - 1) % 2, (G - 1 - G_GA) * NC)
                    if n == 3 and phase < 3 and h >= 4:
                        act.wait_ge(*source_kept(phase + 1, h - 4))
                        lhs_pair(phase + 1, h - 4, (src_a, src_b, src_a)[phase], G)
                    if n == 0 and phase > 0:
                        i = 4 + h if h < 2 or (phase < 3 and h < 4) else h if phase == 3 and h >= 6 else None
                        if i is not None:
                            act.wait_ge(*source_kept(phase, i))
                            lhs_pair(phase, i, (src_a, src_b, src_a)[phase - 1], G - 1)
                    if G_MOBAO < G <= G_OUT and h == 5:
                        k = G - 1 - G_MOBAO
                        act.wait_ge(merge_turned, k + 1)
                        act.activation(src_a[:, 4 * k:4 * k + 4, :], ps[:, 4:6, :].rearrange("p b (k n) -> p (b k) n", k=2),
                                       ACT.Copy).then_inc(merge_kept, 1)
                    if G_MOBAO < G <= G_OUT and h == 0:
                        k = G - 1 - G_MOBAO
                        act.wait_ge(gain_spread, k + 1)
                        act.activation(gain_b[:, k * NC:(k + 1) * NC], ps[:, 6, :], ACT.Copy).then_inc(gain_ready, 1)
                    if G == G_OUT and h == 5:
                        act.wait_ge(gated, 8 + 12)
                        for t in range(T):
                            act.dma_start(x_sb[:, t, :], x[0, t * P:(t + 1) * P, :]).then_inc(x_back, 16)
                    if G > G_OUT and h == 3:
                        square_y(G - 1 - G_OUT, (G - 1) % 2)
                    if G == G_OUT and h == 6:
                        load_root_table()
                group(G, side)

            def up_side(j, par_before):
                def side(h):
                    if h == 3:
                        act.wait_ge(used, 8 * (G_UP + j))
                        wait(act, up_sum, j - 1)
                        act.activation(h_low[:, :, :], ps[:, 4 * par_before:4 * par_before + 4, SEQ:2 * SEQ],
                                       ACT.Copy).then_inc(up_low, 1)
                    if h == 7:
                        act.wait_ge(conv_step, 12 * j)
                        wait(act, g_ready, j - 1)
                        act.activation(a_act[:, :, :], h_conv[:, 0:2, :], ACT.Silu).then_inc(a_ready, 1)
                return side

            def first_up_side(h):
                if h == 2:
                    square_y(3, 1)
                    root_of_norm(1)
                    spare = gT[:, 16:24, :].rearrange("p k n -> p (k n)")
                    for i in range(2 * T):
                        n, t = divmod(i, 2)
                        act.wait_ge(x2_ready, i + 1)
                        wait(act, x2_squared, i)
                        act.activation(spare[:, 0:D // 2], x_sb[:, t, n * D // 2:(n + 1) * D // 2], ACT.Square,
                                       accum_out=squares[:, t, n:n + 1]).then_inc(x2_squared, 1)
                    root_of_norm(2)
                    act.wait_ge(row_spread, 1)
                    act.activation(rstd_row, ps[:, 7, 0:SEQ], ACT.Copy).then_inc(row_ready, 1)
                    act.wait_ge(mod2, 3)
                if h >= 2:
                    for i in (0, 1, 2) if h == 2 else (h,):
                        act.wait_ge(x2_normed, i + 1)
                        for kt in (2 * i, 2 * i + 1):
                            act.activation(gT[:, kt, :], gT[:, kt, :], ACT.Identity, bias=shift2[:, kt:kt + 1],
                                           scale=scale2[:, kt:kt + 1]).then_inc(u2_ready, 1)
                        act.wait_ge(u2_ready, 2 * i + 2)
                        lhs_pair(4, i, gT, G_UP - 1)

            def second_up_side(h):
                if h == 0:
                    act.wait_ge(gain_spread, 5)
                    act.activation(gain_b[:, :].rearrange("p (b n) -> p b n", b=4), ps[:, 4:8, :], ACT.Copy
                                   ).then_inc(gain_ready, 1)
                up_side(1, 0)(h)

            def up_loads(j):
                return G_UP + 2 * j + 2
            group(G_UP, first_up_side, up_loads(0))
            group(G_UP + 1, second_up_side, up_loads(1))
            with act.Fori(1, UPS // 2) as i:
                group(G_UP + 2 * i, up_side(2 * i, 1), up_loads(2 * i))
                group(G_UP + 2 * i + 1, up_side(2 * i + 1, 0), up_loads(2 * i + 1))

            def g_part(kb, i, parity):
                act.wait_ge(g_ready, 2 * kb + i + 1)
                wait(act, used, 8 * (G_DOWN + kb - 1))
                act.activation(g_lhs[:, parity, 2 * i:2 * i + 2, 0:SEQ], gT[:, bass.ds(KB * kb + 2 * i, 2), :], ACT.Copy
                               ).then_inc(g_high, 1)

            def down_side(kb, parity, first=False):
                def side(h):
                    if first and h < 2:
                        g_part(0, h, 0)
                    if first:
                        up_side(UPS, 1)(h)
                    if h in (4, 5):
                        g_part(kb + 1, h - 4, 1 - parity)
                return side

            def down_loads(kb):
                return G_DOWN + UPS + kb + 1
            group(G_DOWN, down_side(0, 0, True), down_loads(0))
            with act.Fori(0, (DOWNS - 3) // 2) as i:
                group(G_DOWN + 2 * i + 1, down_side(2 * i + 1, 1), down_loads(2 * i + 1))
                group(G_DOWN + 2 * i + 2, down_side(2 * i + 2, 0), down_loads(2 * i + 2))
            group(G_DOWN + DOWNS - 2, down_side(DOWNS - 2, 1), down_loads(DOWNS - 2))
            act.wait_ge(root_loaded, 1)
            load_root_table()
            group(G_DOWN + DOWNS - 1, None, down_loads(DOWNS - 1))
            for n in range(4):
                act.wait_ge(used, 8 * (G_DOWN + DOWNS - 1) + 2 * n + 2)
                for t in range(T):
                    wait(act, y2_squared, 2 * n + t)
                    if n == 3 and t == 1:
                        act.wait_ge(y2_gained, 7)
                    act.activation(gT[:, 0:2, :].rearrange("p k n -> p (k n)"), ps[:, 2 * n + t, :], ACT.Square,
                                   accum_out=squares[:, t, n:n + 1]
                                   ).then_inc(y2_squared, 1)
            root_of_norm(3)

        @block.vector
        def _(dve):
            def low_part(n, slot, h):
                dve.wait_ge(high_ready, n + 1)
                dve.tensor_tensor(w_low[:, h % 4, :, :], stage[:, slot, 2 * (h % 2):2 * (h % 2) + 2, :],
                                  w_high[:, h % 4, :, :].bitcast(F32), ALU.subtract).then_inc(split_ready, 1)

            def group(G, side=None, ada=None):
                for h in range(HB):
                    if ada is not None:
                        ada_step_of(*ada, 2 * h)
                    low_part(8 * G + h, h // 2, h)
                    if ada is not None:
                        ada_step_of(*ada, 2 * h + 1)
                    if side is not None:
                        side(h)

            def ada_step_of(j, parity, i):
                b = i // KB
                if i % KB == 0:
                    dve.wait_ge(ada_in[b % 2], 16 * (2 * j + b // 2 + 1))
                block_, acc = ada_ring[:, b % 2, i % KB, :], ada_acc[:, parity, :]
                if i == 0:
                    if not (isinstance(j, int) and j < 2):
                        dve.wait_ge(ada_summed, j - 1)
                    op = dve.tensor_scalar(acc, block_, c_act[:, 0:1], None, ALU.mult)
                else:
                    dve.wait_ge(ada_step, 16 * j + i)
                    op = dve.scalar_tensor_tensor(out=acc, in0=block_, scalar=c_act[:, i:i + 1], in1=acc,
                                                  op0=ALU.mult, op1=ALU.add)
                op.then_inc(ada_step, 1)

            def keep_chunk(j):
                dve.wait_ge(ada_summed, j + 1)
                dve.tensor_copy(ada_cols[:, bass.ds(2 * j, 2)], ps[:, 7, 0:2]).then_inc(ada_kept, 1)

            def lhs_pair(phase, i, src):
                dve.wait_ge(lhs_high, 8 * phase + i + 1)
                dve.tensor_tensor(lhs[:, 2 * i:2 * i + 2, SEQ:2 * SEQ], src[:, 2 * i:2 * i + 2, :],
                                  lhs[:, 2 * i:2 * i + 2, 0:SEQ].bitcast(F32), ALU.subtract).then_inc(lhs_ready, 1)

            def mean_of(k, parts):
                src = squares[:, :, 0]
                if parts > 1:
                    dve.tensor_reduce(mean_sq[:, :], squares[:, :, 0:parts], AX.X, ALU.add).then_inc(norm_sum, 1)
                    dve.wait_ge(norm_sum, k)
                    src = mean_sq[:, :]
                dve.tensor_scalar(rstd[:, :], src, 1.0 / D, NORM_EPS, ALU.mult, ALU.add).then_inc(norm_mean, 1)

            def inverse_root(k):
                dve.wait_ge(norm_root, k + 1)
                dve.reciprocal(rstd[:, :], rstd[:, :]).then_inc(norm_inv, 1)

            def rstd_of(k, parts):
                mean_of(k, parts)
                inverse_root(k)
                dve.wait_ge(norm_inv, k + 1)

            dve.wait_ge(cols_ready, 2)

            def first_chunk(kb, which, n, between):
                for i in range(KT):
                    if i % KB == 0:
                        dve.wait_ge(ada1_in[i // KB], 16 * (n + 1))
                    block_, acc = ada_first[:, i // KB, i % KB, :], ada_acc1[:, which, i % 2, :]
                    if i < 2:
                        wait(dve, ada1_summed, n - 1)
                        op = dve.tensor_scalar(acc, block_, c_act[:, i:i + 1], None, ALU.mult)
                    else:
                        dve.wait_ge(ada1_step, KT * n + i - 1)
                        op = dve.scalar_tensor_tensor(out=acc, in0=block_, scalar=c_act[:, i:i + 1], in1=acc,
                                                      op0=ALU.mult, op1=ALU.add)
                    op.then_inc(ada1_step, 1)
                    if i in between:
                        between[i]()

            def late_low_part(kb, i):
                n = 2 * G_FIRST * kb + 4 + i
                low_part(n, n // 2 % 4, n)

            def first_shift(kb):
                here = shift1[:, KB * kb:KB * kb + KB]
                dve.wait_ge(ada1_summed, 2 * kb + 1)
                dve.tensor_tensor(here, ps[:, 6, 0:KB], cols[:, 3 * KT + KB * kb:3 * KT + KB * kb + KB], ALU.add
                                  ).then_inc(ada1_cols, 1)

            def first_scale(kb):
                here = scale1[:, KB * kb:KB * kb + KB]
                dve.wait_ge(ada1_summed, 2 * kb + 2)
                dve.scalar_tensor_tensor(out=here, in0=ps[:, 7, 0:KB], scalar=1.0,
                                         in1=cols[:, 4 * KT + KB * kb:4 * KT + KB * kb + KB], op0=ALU.add, op1=ALU.add
                                         ).then_inc(ada1_cols, 1)
                dve.wait_ge(ada1_cols, 2 * kb + 2)
                dve.tensor_tensor(here, here, cols[:, KT + KB * kb:KT + KB * kb + KB], ALU.mult).then_inc(scale1_ready, 1)
                dve.wait_ge(scale1_ready, kb + 1)

            for kb in range(KT // KB):
                late = {3: lambda: late_low_part(kb - 1, 0), 7: lambda: late_low_part(kb - 1, 1)}
                first_chunk(kb, 0, 2 * kb, late if kb else {})
                if kb == 0:
                    dve.wait_ge(squared, 2)
                    mean_of(0, 1)
                    inverse_root(0)
                first_chunk(kb, 1, 2 * kb + 1, {7: lambda: first_shift(kb)})
                for n in range(2 * G_FIRST * kb, 2 * G_FIRST * kb + 2):
                    low_part(n, n // 2 % 4, n)
                first_scale(kb)
                if kb == 0:
                    dve.wait_ge(xT_ready, 8)
                for kt in range(KB * kb, KB * kb + KB):
                    dve.tensor_scalar(src_b[:, kt, :], src_a[:, kt, :], scale1[:, kt:kt + 1],
                                      shift1[:, kt:kt + 1], ALU.mult, ALU.add).then_inc(u_ready, 1)
                for i in range(2):
                    lhs_pair(0, 2 * kb + i, src_b)
                for n in range(2 * G_FIRST * kb + 2, 2 * G_FIRST * kb + 4):
                    low_part(n, n // 2 % 4, n)
            for i in range(2):
                late_low_part(KT // KB - 1, i)
            dve.wait_ge(consts_in, 48)
            dve.wait_ge(cols_ready, 4)

            def rotate(n, t, bank, done):
                i = 2 * n + t
                src = ps[:, bank + t, :].rearrange("p (h d) -> p h d", h=SETH)
                r_cos, r_sin = (r[:, :].rearrange("p (h d) -> p h d", h=SETH) for r in (rot_cos, rot_sin))
                half = RET_DK // 2
                dve.wait_ge(used, done)
                wait(dve, rot_ready, i)
                dve.tensor_tensor(r_cos, src, cos2[:, t, :].unsqueeze(1).broadcast_to([P, SETH, P]), ALU.mult
                                  ).then_inc(rot_terms, 1)
                for a, b in ((0, half), (half, 0)):
                    dve.tensor_tensor(r_sin[:, :, a:a + half], src[:, :, b:b + half],
                                      sin2[:, t, a:a + half].unsqueeze(1).broadcast_to([P, SETH, half]), ALU.mult
                                      ).then_inc(rot_terms, 1)
                dve.wait_ge(rot_terms, 3 * i + 3)
                wait(dve, rqk_turned, n - 1)
                dve.tensor_tensor(rot[:, n % 2, t, :], rot_cos[:, :], rot_sin[:, :], ALU.add).then_inc(rot_ready, 1)

            def head_outs():
                return [(hd, t, ps[:, 4 + hd, t * RET_DV:(t + 1) * RET_DV]) for hd in range(2) for t in range(T)]

            def norm_heads(s, i):
                n = 2 * s + i
                dve.wait_ge(ret_summed, n + 1)
                outs = head_outs()
                for k, (hd, t, o) in enumerate(outs):
                    dve.bn_stats(stats[:, k, :], o).then_inc(gn_stats, 1)
                for k in range(4):
                    dve.wait_ge(gn_stats, 4 * n + k + 1)
                    dve.bn_aggr(moments[:, k, :], stats[:, k, :]).then_inc(gn_moments, 1)
                dve.wait_ge(gn_moments, 4 * n + 4)
                dve.tensor_scalar(inv_std[:, :], moments[:, :, 1], GN_EPS, None, ALU.add).then_inc(gn_var, 1)

            def scale_heads(s, i):
                n = 2 * s + i
                outs = head_outs()
                dve.wait_ge(gn_root, n + 1)
                dve.reciprocal(inv_std[:, :], inv_std[:, :]).then_inc(gn_inv, 1)
                dve.wait_ge(gn_inv, n + 1)
                wait(dve, ret_turned, n - 1)
                for k, (hd, t, o) in enumerate(outs):
                    at = (2 * i + hd) * RET_DV
                    dve.tensor_scalar(o_ret[:, t, at:at + RET_DV], o, moments[:, k, 0:1], inv_std[:, k:k + 1],
                                      ALU.subtract, ALU.mult).then_inc(gn_ready, 1)

            def ret_side(G):
                def side(h):
                    if h == 6 and G > G_FIRST:
                        keep_chunk(G - 1 - G_FIRST)
                    if G == G_FIRST and 1 <= h <= 4:
                        n = (h - 1) // 2
                        rotate(n, (h - 1) % 2, FIRST_BANKS[1 + n], 8 * G_FIRST - 2 + 2 * n)
                    for s in range(RET_SETS):
                        g = G - 6 * s
                        if s and g in (1, 2) and h in (3, 4):
                            rotate(2 * s + g - 1, h - 3, 2 * ((G - 1) % 2), 8 * G)
                        if (g, h) == (4, 5):
                            dve.wait_ge(ret_scored, s + 1)
                            wait(dve, ret_summed, 2 * s)
                            if s == 0:
                                dve.wait_ge(decay_in, 16)
                            dec = decay[:, SETH * s:SETH * s + SETH, :]
                            dve.tensor_tensor(sT0[:, :, :], ps[:, 5:7, :].rearrange("p b (h n) -> p (b h) n", h=2), dec,
                                              ALU.mult).then_inc(ret_decayed, 1)
                            dve.tensor_tensor(sT1[:, :, :], ps[:, 4, :].rearrange("p (h n) -> p h n", h=SETH),
                                              dec[:, :, 0:P], ALU.mult).then_inc(ret_decayed, 1)
                        if (g, h) == (5, 0):
                            norm_heads(s, 0)
                        if (g, h) == (5, 1):
                            scale_heads(s, 0)
                        if (g, h) == (5, 5):
                            norm_heads(s, 1)
                        if (g, h) == (5, 6):
                            scale_heads(s, 1)
                        if (g, h) in ((5, 4), (6, 4)):
                            n = 2 * s + g - 5
                            dve.wait_ge(rg_ready, n + 1)
                            dve.wait_ge(gn_ready, 4 * n + 4)
                            o = o_ret[:, :, (g - 5) * NC:(g - 4) * NC]
                            dve.tensor_tensor(o, o, gate_r[:, :, :], ALU.mult).then_inc(ret_gated, 1)
                return side

            for G in range(G_FIRST, G_MOBA):
                group(G, ret_side(G), (G - G_FIRST, (G + 1) % 2))

            def moba_set(s, first):
                def side_of(g):
                    ret = ret_side(G_MOBA) if first and g == 0 else None

                    def side(h):
                        if ret is not None:
                            ret(h)
                        elif h == 6:
                            keep_chunk(G_MOBA + 4 * s + g - 1 - G_FIRST)
                        if (g, h) == (3, 0):
                            dve.wait_ge(scored, s + 1)
                            if not first:
                                dve.wait_ge(probs_turned, s)
                            scale = 1.0 / math.sqrt(MOBA_HD)
                            dve.scalar_tensor_tensor(
                                out=p0[:, :, :], in0=ps[:, 4, :].rearrange("p (h n) -> p h n", h=SETH), scalar=scale,
                                in1=mask[:, 0:P].unsqueeze(1).broadcast_to([P, SETH, P]),
                                op0=ALU.mult, op1=ALU.add).then_inc(masked, 1)
                            dve.scalar_tensor_tensor(
                                out=p1[:, :, :], in0=ps[:, 5:7, :].rearrange("p b (h n) -> p (b h) n", h=2), scalar=scale,
                                in1=mask[:, P:3 * P].unsqueeze(1).broadcast_to([P, SETH, SEQ]),
                                op0=ALU.mult, op1=ALU.add).then_inc(masked, 1)
                        if (g, h) == (3, 1):
                            dve.wait_ge(masked, 2 * s + 2)
                            dve.tensor_reduce(row_max[:, 0:SETH], p0[:, :, :], AX.X, ALU.max).then_inc(maxed, 1)
                            dve.tensor_reduce(row_max[:, SETH:2 * SETH], p1[:, :, :], AX.X, ALU.max).then_inc(maxed, 1)
                            dve.wait_ge(maxed, 2 * s + 2)
                            dve.tensor_scalar(neg_max[:, :], row_max[:, :], -1.0, None, ALU.mult).then_inc(neg_ready, 1)
                        if (g, h) == (3, 4):
                            dve.wait_ge(exp_ready, 8 * s + 8)
                            dve.reciprocal(inv_sum[:, :], row_sum[:, :]).then_inc(inv_ready, 1)
                            dve.wait_ge(inv_ready, s + 1)
                            dve.tensor_tensor(p0[:, :, :], p0[:, :, :],
                                              inv_sum[:, 0:SETH].unsqueeze(2).broadcast_to([P, SETH, P]), ALU.mult
                                              ).then_inc(probs_ready, 1)
                            dve.tensor_tensor(p1[:, :, :], p1[:, :, :],
                                              inv_sum[:, SETH:2 * SETH].unsqueeze(2).broadcast_to([P, SETH, SEQ]), ALU.mult
                                              ).then_inc(probs_ready, 1)
                    return side
                for g in range(4):
                    group(G_MOBA + 4 * s + g, side_of(g), (G_MOBA + 4 * s + g - G_FIRST, (g + 1) % 2))

            moba_set(0, True)
            with dve.Fori(1, MOBA_SETS) as s:
                moba_set(s, False)

            def gain_y(n, parity):
                dve.wait_ge(used, 8 * (G_OUT + n + 1))
                dve.wait_ge(gain_ready, n + 1)
                for t in range(T) if n < 3 else (1, 0):
                    if n < 3 or t == 0:
                        dve.wait_ge(y_squared, 2 * n + t + 1)
                    dve.tensor_tensor(y_gain[:, t, n * NC:(n + 1) * NC], ps[:, 2 * parity + t, :],
                                      gain_b[:, n * NC:(n + 1) * NC], ALU.mult).then_inc(y_gained, 1)

            def gain_column(which):
                a = (0, 3 * KT)[which]
                dve.scalar_tensor_tensor(out=gain[:, :], in0=ada_cols[:, a:a + KT], scalar=1.0,
                                         in1=post_cols[:, (2 + which) * KT:(3 + which) * KT], op0=ALU.add, op1=ALU.add
                                         ).then_inc(gain_col, 1)
                dve.wait_ge(gain_col, 4 * which + 1)
                dve.tensor_tensor(gain[:, :], gain[:, :], post_cols[:, which * KT:(which + 1) * KT], ALU.mult
                                  ).then_inc(gain_col, 1)
                dve.wait_ge(gain_col, 4 * which + 2)
                dve.tensor_copy(gain_high[:, :], gain[:, :]).then_inc(gain_col, 1)
                dve.wait_ge(gain_col, 4 * which + 3)
                dve.tensor_tensor(gain_low[:, :], gain[:, :], gain_high[:, :].bitcast(F32), ALU.subtract
                                  ).then_inc(gain_col, 1)
                dve.wait_ge(gain_col, 4 * which + 4)

            def diagonal(diag, n, i, tile):
                for part, column in enumerate((gain_high, gain_low)):
                    at = (2 * n + part) * NC + i * P
                    dve.tensor_scalar(diag[:, at:at + P], ident[:, :], column[:, tile:tile + 1].bitcast(F32), None,
                                      ALU.mult).then_inc(gain_diag, 1)

            for G in range(G_GA, G_UP):
                phase, n = divmod(G - G_GA, 4)

                def side(h):
                    if h == 6 and G <= G_FIRST + ADA_CHUNKS:
                        keep_chunk(G - 1 - G_FIRST)
                    if G_RETO < G <= G_MOBAO and h == 3:
                        k = G - 1 - G_RETO
                        dve.wait_ge(used, 8 * G)
                        dve.wait_ge(gate_ready, 2 * MOBA_SETS + 2 * k + 2)
                        for t in range(T):
                            a = gate_a[:, t, k * NC:(k + 1) * NC]
                            dve.tensor_tensor(a, a, ps[:, 2 * ((G - 1) % 2) + t, :], ALU.mult).then_inc(gated, 1)
                    if G_MOBAO < G <= G_OUT and h == 3:
                        k = G - 1 - G_MOBAO
                        dve.wait_ge(used, 8 * G)
                        for t in range(T):
                            b = gate_b[:, t, k * NC:(k + 1) * NC]
                            dve.tensor_tensor(b, b, ps[:, 2 * ((G - 1) % 2) + t, :], ALU.mult).then_inc(gated, 1)
                        dve.wait_ge(gated, 8 + 3 * k + 2)
                        a = gate_a[:, :, k * NC:(k + 1) * NC]
                        dve.tensor_tensor(a, a, gate_b[:, :, k * NC:(k + 1) * NC], ALU.add).then_inc(gated, 1)
                    if n == 3 and phase < 3 and h >= 4:
                        lhs_pair(phase + 1, h - 4, (src_a, src_b, src_a)[phase])
                    if n == 0 and phase > 0:
                        src = (src_a, src_b, src_a)[phase - 1]
                        if (phase < 3 and h < 4) or (phase == 3 and h < 2):
                            lhs_pair(phase, 4 + h, src)
                        if phase == 3 and h >= 6:
                            lhs_pair(phase, h, src)
                    if G == G_MOBAO and h == 4:
                        dve.wait_ge(ada_kept, ADA_CHUNKS)
                        dve.tensor_copy(ones_r[:, :], ones[:, :])
                        gain_column(0)
                    if G_MOBAO <= G < G_OUT and h == 5:
                        k = G - G_MOBAO
                        wait(dve, gain_spread, k - 1)
                        for i in range(4):
                            diagonal(diag1, k % 2, i, 4 * k + i)
                    if G == G_OUT and h == 4:
                        dve.tensor_tensor(shift2[:, :], ada_cols[:, KT:2 * KT], cols[:, 5 * KT:6 * KT], ALU.add
                                          ).then_inc(mod2, 1)
                        dve.scalar_tensor_tensor(out=scale2[:, :], in0=ada_cols[:, 2 * KT:3 * KT], scalar=1.0,
                                                 in1=cols[:, 6 * KT:7 * KT], op0=ALU.add, op1=ALU.add).then_inc(mod2, 1)
                        dve.wait_ge(mod2, 2)
                        dve.tensor_tensor(scale2[:, :], scale2[:, :], cols[:, 2 * KT:3 * KT], ALU.mult).then_inc(mod2, 1)
                    if G > G_OUT and h == 3:
                        gain_y(G - 1 - G_OUT, (G - 1) % 2)
                    if G > G_OUT and h == 5:
                        if G == G_OUT + 1:
                            dve.wait_ge(gain_spread, 4)
                            gain_column(1)
                        k = G - 1 - G_OUT
                        for i in range(16 * k // 3, 16 * (k + 1) // 3):
                            diagonal(diag2, i // 4, i % 4, i)
                group(G, side, (G - G_FIRST, (G + 1) % 2) if G < G_FIRST + ADA_CHUNKS else None)

            def conv(out_, c, tile, shift, add):
                src = h_pad[:, c, 2 - shift:2 - shift + SEQ]
                tap = conv_cols[:, 2 - shift, bass.ds(tile, 1)]
                if add is None:
                    return dve.tensor_scalar(out_, src, tap, conv_cols[:, 3, bass.ds(tile, 1)], ALU.mult, ALU.add)
                return dve.scalar_tensor_tensor(out=out_, in0=src, scalar=tap, in1=add, op0=ALU.mult, op1=ALU.add)

            def up_side(j, par_before):
                def side(h):
                    if h == 3:
                        dve.wait_ge(up_low, j)
                        wait(dve, conv_step, 12 * (j - 1))
                        dve.tensor_tensor(h_pad[:, :, 2:2 + SEQ], ps[:, 4 * par_before:4 * par_before + 4, 0:SEQ],
                                          h_low[:, :, :], ALU.add).then_inc(up_sum, 1)
                    if h in (4, 5, 6):
                        if h == 4:
                            dve.wait_ge(up_sum, j)
                            wait(dve, g_ready, j - 1)
                            if isinstance(j, int) and j == 1:
                                dve.wait_ge(pad_set, 1)
                        for c in range(4):
                            tile = 2 * (j - 1) + c % 2 + (c // 2) * (D_FF // P)
                            acc = h_conv[:, c, :]
                            if h > 4:
                                dve.wait_ge(conv_step, 12 * (j - 1) + 4 * (h - 5) + c + 1)
                            conv(acc, c, tile, h - 4, None if h == 4 else acc).then_inc(conv_step, 1)
                    if h == 7:
                        dve.wait_ge(a_ready, j)
                        dve.tensor_tensor(gT[:, bass.ds(2 * (j - 1), 2), :], a_act[:, :, :], h_conv[:, 2:4, :], ALU.mult
                                          ).then_inc(g_ready, 1)
                return side

            def norm_pair(i):
                dve.wait_ge(x2_turned, i + 1)
                dve.tensor_tensor(gT[:, 2 * i:2 * i + 2, :], ps[:, 4 + i % 4, :].rearrange("p (k n) -> p k n", k=2),
                                  rstd_row.unsqueeze(1).broadcast_to([P, 2, SEQ]), ALU.mult).then_inc(x2_normed, 1)

            def first_up_side(h):
                if h == 2:
                    gain_y(3, 1)
                    dve.wait_ge(y_squared, 8)
                    rstd_of(1, 4)
                    dve.wait_ge(y_gained, 8)
                    dve.wait_ge(x_back, 32)
                    for n in range(2):
                        for t in range(T):
                            half = slice(n * D // 2, (n + 1) * D // 2)
                            dve.scalar_tensor_tensor(out=x_sb[:, t, half], in0=y_gain[:, t, half], scalar=rstd[:, t:t + 1],
                                                     in1=x_sb[:, t, half], op0=ALU.mult, op1=ALU.add).then_inc(x2_ready, 1)
                    dve.wait_ge(x2_squared, 4)
                    rstd_of(2, 2)
                    for t in range(T):
                        dve.tensor_scalar(diag_rstd[:, t * P:(t + 1) * P], ident[:, :], rstd[:, t:t + 1], None, ALU.mult
                                          ).then_inc(rstd_diag, 1)
                    dve.wait_ge(row_ready, 1)
                    norm_pair(0)
                    norm_pair(1)
                    lhs_pair(4, 0, gT)
                    norm_pair(2)
                    lhs_pair(4, 1, gT)
                    norm_pair(3)
                    lhs_pair(4, 2, gT)
                if h > 2:
                    if h < 7:
                        norm_pair(h + 1)
                    lhs_pair(4, h, gT)

            def second_up_side(h):
                if h == 3:
                    dve.wait_ge(x2_turned, 8)
                    dve.memset(h_pad[:, :, 0:2], 0.0).then_inc(pad_set, 1)
                up_side(1, 0)(h)

            group(G_UP, first_up_side)
            group(G_UP + 1, second_up_side)
            with dve.Fori(1, UPS // 2) as i:
                group(G_UP + 2 * i, up_side(2 * i, 1))
                group(G_UP + 2 * i + 1, up_side(2 * i + 1, 0))

            def g_part(kb, i, parity):
                dve.wait_ge(g_high, 2 * kb + i + 1)
                dve.tensor_tensor(g_lhs[:, parity, 2 * i:2 * i + 2, SEQ:2 * SEQ], gT[:, bass.ds(KB * kb + 2 * i, 2), :],
                                  g_lhs[:, parity, 2 * i:2 * i + 2, 0:SEQ].bitcast(F32), ALU.subtract).then_inc(g_split, 1)

            def down_side(kb, parity, first=False):
                def side(h):
                    if first and h < 2:
                        g_part(0, h, 0)
                    if first:
                        up_side(UPS, 1)(h)
                    if h in (4, 5):
                        g_part(kb + 1, h - 4, 1 - parity)
                return side

            group(G_DOWN, down_side(0, 0, True))
            with dve.Fori(0, (DOWNS - 3) // 2) as i:
                group(G_DOWN + 2 * i + 1, down_side(2 * i + 1, 1))
                group(G_DOWN + 2 * i + 2, down_side(2 * i + 2, 0))
            group(G_DOWN + DOWNS - 2, down_side(DOWNS - 2, 1))
            group(G_DOWN + DOWNS - 1)
            dve.wait_ge(g_ready, UPS)
            for n in range(4):
                dve.wait_ge(used, 8 * (G_DOWN + DOWNS - 1) + 2 * n + 2)
                if n == 0:
                    dve.wait_ge(gain_ready, 5)
                for t in range(T) if n < 3 else (1, 0):
                    if n < 3 or t == 0:
                        dve.wait_ge(y2_squared, 2 * n + t + 1)
                    dve.tensor_tensor(y_gain[:, t, n * NC:(n + 1) * NC], ps[:, 2 * n + t, :],
                                      gain_b[:, n * NC:(n + 1) * NC], ALU.mult).then_inc(y2_gained, 1)
            dve.wait_ge(y2_squared, 8)
            rstd_of(3, 4)
            dve.wait_ge(y2_gained, 8)
            for t in range(T):
                for n in range(4):
                    o = y_gain[:, t, n * NC:(n + 1) * NC]
                    dve.scalar_tensor_tensor(out=o, in0=o, scalar=rstd[:, t:t + 1], in1=x_sb[:, t, n * NC:(n + 1) * NC],
                                             op0=ALU.mult, op1=ALU.add).then_inc(out_ready, 1)


def kernel(**inputs):
    import concourse.bacc as bacc
    from concourse.bass_utils import run_bass_kernel_spmd

    names = ["x", "c", "ada_w", "ada_b", "mix_norm_pre", "mix_norm_post", "w_in", "ret_w_o", "moba_w_o", "w_out",
             "ffn_norm_pre", "ffn_norm_post", "ffn_w_up", "ffn_conv_w", "ffn_conv_b", "ffn_w_down"]
    half = RET_DK // 2
    angle = (np.arange(SEQ, dtype=np.float32)[:, None]
             * (ROPE_BASE ** (-np.arange(half, dtype=np.float32) / half)).astype(np.float32)[None, :])
    by_tile = lambda a: np.ascontiguousarray(a.reshape(T, P, P).transpose(1, 0, 2)).astype(np.float32)
    cos, sin = np.cos(angle), np.sin(angle)
    diff = np.arange(SEQ)[None, :] - np.arange(P)[:, None]
    log_g = np.log1p(-np.exp2(-5.0 - np.arange(RET_HEADS)))
    decay = np.where(diff[:, None, :] >= 0, np.exp(np.maximum(diff, 0)[:, None, :] * log_g[None, :, None]), 0.0)
    tri = np.where(np.arange(P)[None, :] <= np.arange(P)[:, None], 0.0, MASKED)
    tables = {
        "identity": np.eye(P, dtype=np.float32),
        "rope_cos": by_tile(np.concatenate([cos, cos], axis=1)),
        "rope_sin": by_tile(np.concatenate([-sin, sin], axis=1)),
        "causal": np.concatenate([tri, np.zeros((P, P)), tri], axis=1).astype(np.float32),
        "decay": (decay * RET_DK ** -0.5).astype(np.float32),
    }
    nc = bacc.Bacc("TRN2", target_bir_lowering=False, num_devices=1)
    arrays, args = {}, []
    for name in names:
        arrays[f"in_{name}"] = np.ascontiguousarray(inputs[name])
    arrays.update({f"table_{k}": v for k, v in tables.items()})
    for name, a in arrays.items():
        args.append(nc.dram_tensor(name, a.shape, mybir.dt.from_np(a.dtype), kind="ExternalInput").ap())
    args.append(nc.dram_tensor("out", (1, SEQ, D), F32, kind="ExternalOutput").ap())
    hybrid_block(nc, *args)
    result = run_bass_kernel_spmd(nc, [arrays], core_ids=[0])
    return result.results[0]["out"]
```
